# Optimizing a Trainium2 kernel written in Bass

```python
import math
import jax
import jax.numpy as jnp
from jax import lax
import numpy as np

D_MODEL = 1024
BATCH = 1
SEQ = 512
DEPTH = 2
DEC_BATCH = 8
DEC_SEQ = 4
PAST_LEN = 2048
PAGE_SIZE = 128

N_MIXERS = 2
N_NSA_LAYERS = (DEPTH + N_MIXERS - 1) // N_MIXERS
N_SSD_LAYERS = DEPTH // N_MIXERS

NSA_HEADS = 16
NSA_HEAD_DIM = D_MODEL // NSA_HEADS
NSA_KV_GROUPS = 4
NSA_GROUP_SIZE = NSA_HEADS // NSA_KV_GROUPS
CMP_BLOCK = 32
CMP_STRIDE = 16
CMP_OVERLAP = CMP_BLOCK // CMP_STRIDE
CMP_HIDDEN = 4 * NSA_HEAD_DIM
SEL_BLOCK = 64
SEL_CHUNKS = SEL_BLOCK // CMP_STRIDE
SEL_TOPN = 16
WINDOW = 512
NSA_QUERY_BLOCK = 32
NSA_Q_DIM = NSA_HEADS * NSA_HEAD_DIM
NSA_KV_DIM = 2 * NSA_KV_GROUPS * NSA_HEAD_DIM
NSA_IN = NSA_Q_DIM + 3 * NSA_KV_DIM + 3 * NSA_HEADS

SSM_EXPAND = 2
SSM_D_INNER = SSM_EXPAND * D_MODEL
SSM_HEAD_DIM = 64
SSM_HEADS = SSM_D_INNER // SSM_HEAD_DIM
SSM_GROUPS = 4
SSM_HEADS_PER_GROUP = SSM_HEADS // SSM_GROUPS
SSM_STATE = 128
SSM_CONV = 4
SSM_CONV_DIM = SSM_D_INNER + 2 * SSM_GROUPS * SSM_STATE
SSM_IN = SSM_D_INNER + SSM_CONV_DIM + SSM_HEADS
SSM_CHUNK = 128

FFN_HIDDEN = -(-(8 * D_MODEL) // (3 * 256)) * 256

NORM_EPS = 1e-6
NEG_INF = -1e30
FORCE_SCORE = 1e4

kernel_name = "nsa_mamba2_hybrid_decode_step"

def rms_norm(x, g):
    xf = x.astype(jnp.float32)
    y = xf * lax.rsqrt(jnp.mean(xf * xf, axis=-1, keepdims=True) + NORM_EPS)
    return (y * g.astype(jnp.float32)).astype(x.dtype)

def masked_softmax(logits, mask):
    logits = jnp.where(mask, logits, NEG_INF)
    return jnp.where(mask, jax.nn.softmax(logits, axis=-1), 0.0)

def alibi_slopes(n):
    start = 2.0 ** (-8.0 / n)
    return jnp.asarray(start ** np.arange(1, n + 1), dtype=jnp.float32)

def swiglu(h, w_gate, w_up, w_down):
    return (jax.nn.silu(h @ w_gate) * (h @ w_up)) @ w_down

def gather_pages(pool, page_table):
    pages = pool[page_table]
    b, n_pages = page_table.shape
    return pages.reshape((b, n_pages * PAGE_SIZE) + pages.shape[3:])

def compress_blocks(rows, pe, w1, w2):
    b, t = rows.shape[0], rows.shape[1]
    n_chunk = t // CMP_STRIDE
    n_blk = n_chunk - CMP_OVERLAP + 1
    chunks = rows[:, : n_chunk * CMP_STRIDE].reshape(b, n_chunk, CMP_STRIDE, NSA_KV_GROUPS, NSA_HEAD_DIM)
    pe = pe.reshape(CMP_OVERLAP, CMP_STRIDE, NSA_HEAD_DIM).astype(rows.dtype)
    w1 = w1.reshape(CMP_OVERLAP, CMP_STRIDE, NSA_HEAD_DIM, CMP_HIDDEN)
    pre = 0.0
    for m in range(CMP_OVERLAP):
        part = jnp.einsum("bcjgd,jdh->bcgh", chunks + pe[m][None, None, :, None, :], w1[m])
        pre = pre + part[:, m:m + n_blk]
    return jnp.einsum("bngh,hd->bngd", jax.nn.silu(pre), w2)

def nsa_attend(q, q_pos, kc, vc, ks, vs, kw, vw, kw_pos):
    b, t = q.shape[0], q.shape[1]
    f32 = jnp.float32
    qb = NSA_QUERY_BLOCK if t % NSA_QUERY_BLOCK == 0 else t
    n_qblk = t // qb
    span = kw.shape[1] - (n_qblk - 1) * qb
    n_cmp = kc.shape[1]
    n_chunk = n_cmp + CMP_OVERLAP - 1
    kc_pos = jnp.arange(n_cmp, dtype=jnp.int32) * CMP_STRIDE + (CMP_BLOCK - 1)
    t_k = ks.shape[1]
    n_sel = -(-t_k // SEL_BLOCK)
    top_n = min(SEL_TOPN, n_sel)
    pad = n_sel * SEL_BLOCK - t_k

    def to_blocks(r):
        r = jnp.pad(r, ((0, 0), (0, pad), (0, 0), (0, 0)))
        r = r.reshape(b, n_sel, SEL_BLOCK, NSA_KV_GROUPS, NSA_HEAD_DIM)
        return r.transpose(0, 3, 1, 2, 4)

    ks_blk = to_blocks(ks)
    vs_blk = to_blocks(vs)
    gather = jax.vmap(jax.vmap(lambda blocks, idx: blocks[idx]))
    slopes = alibi_slopes(NSA_HEADS).reshape(NSA_KV_GROUPS, NSA_GROUP_SIZE)
    scale = NSA_HEAD_DIM ** -0.5
    blk_ids = jnp.arange(n_sel, dtype=jnp.int32)
    in_blk = jnp.arange(SEL_BLOCK, dtype=jnp.int32)

    def block_fn(i):
        q0 = i * qb
        qg = lax.dynamic_slice_in_dim(q, q0, qb, axis=1).reshape(b, qb, NSA_KV_GROUPS, NSA_GROUP_SIZE, NSA_HEAD_DIM)
        tq = lax.dynamic_slice_in_dim(q_pos, q0, qb)
        dist_c = tq[:, None] - kc_pos[None, :]
        lc = (jnp.einsum("bqgrd,bngd->bqgrn", qg, kc).astype(f32) * scale
              - slopes[None, None, :, :, None] * dist_c[None, :, None, None, :].astype(f32))
        pc = masked_softmax(lc, (dist_c >= 0)[None, :, None, None, :])
        o_c = jnp.einsum("bqgrn,bngd->bqgrd", pc.astype(vc.dtype), vc)
        imp = jnp.pad(pc.sum(axis=3), ((0, 0), (0, 0), (0, 0), (CMP_OVERLAP - 1, CMP_OVERLAP - 1)))
        p_chunk = 0.0
        for n in range(CMP_OVERLAP):
            p_chunk = p_chunk + imp[..., CMP_OVERLAP - 1 - n: CMP_OVERLAP - 1 - n + n_chunk]
        p_chunk = jnp.pad(p_chunk, ((0, 0), (0, 0), (0, 0), (0, n_sel * SEL_CHUNKS - n_chunk)))
        p_slc = p_chunk.reshape(b, qb, NSA_KV_GROUPS, n_sel, SEL_CHUNKS).sum(axis=-1)
        cur = tq // SEL_BLOCK
        forced = (blk_ids[None] == 0) | (blk_ids[None] == cur[:, None]) | (blk_ids[None] == cur[:, None] - 1)
        visible = blk_ids[None] * SEL_BLOCK <= tq[:, None]
        score = jnp.where(forced[None, :, None], FORCE_SCORE, jnp.where(visible[None, :, None], p_slc, -1.0))
        _, sel = lax.top_k(score, top_n)
        sel_t = sel.transpose(0, 2, 1, 3).reshape(b, NSA_KV_GROUPS, qb * top_n)
        k_sel = gather(ks_blk, sel_t).reshape(b, NSA_KV_GROUPS, qb, top_n, SEL_BLOCK, NSA_HEAD_DIM)
        v_sel = gather(vs_blk, sel_t).reshape(b, NSA_KV_GROUPS, qb, top_n, SEL_BLOCK, NSA_HEAD_DIM)
        s_pos = sel[..., None] * SEL_BLOCK + in_blk
        dist_s = tq[None, :, None, None, None] - s_pos
        ls = (jnp.einsum("bqgrd,bgqksd->bqgrks", qg, k_sel).astype(f32) * scale
              - slopes[None, None, :, :, None, None] * dist_s[:, :, :, None].astype(f32))
        ps = masked_softmax(ls.reshape(b, qb, NSA_KV_GROUPS, NSA_GROUP_SIZE, top_n * SEL_BLOCK),
                            (dist_s >= 0).reshape(b, qb, NSA_KV_GROUPS, 1, top_n * SEL_BLOCK))
        ps = ps.reshape(b, qb, NSA_KV_GROUPS, NSA_GROUP_SIZE, top_n, SEL_BLOCK)
        o_s = jnp.einsum("bqgrks,bgqksd->bqgrd", ps.astype(vs.dtype), v_sel)
        kwb = lax.dynamic_slice_in_dim(kw, q0, span, axis=1)
        vwb = lax.dynamic_slice_in_dim(vw, q0, span, axis=1)
        wpos = lax.dynamic_slice_in_dim(kw_pos, q0, span)
        dist_w = tq[:, None] - wpos[None, :]
        mask_w = (dist_w >= 0) & (dist_w < WINDOW) & (wpos[None, :] >= 0)
        lw = (jnp.einsum("bqgrd,bsgd->bqgrs", qg, kwb).astype(f32) * scale
              - slopes[None, None, :, :, None] * dist_w[None, :, None, None, :].astype(f32))
        pw = masked_softmax(lw, mask_w[None, :, None, None, :])
        o_w = jnp.einsum("bqgrs,bsgd->bqgrd", pw.astype(vw.dtype), vwb)
        shp = (b, qb, NSA_HEADS, NSA_HEAD_DIM)
        return (o_c.reshape(shp), o_s.reshape(shp), o_w.reshape(shp))

    o_c, o_s, o_w = lax.map(block_fn, jnp.arange(n_qblk))
    def unblock(o):
        return o.transpose(1, 0, 2, 3, 4).reshape(b, t, NSA_HEADS, NSA_HEAD_DIM)
    return unblock(o_c), unblock(o_s), unblock(o_w)

def nsa_layer(h, past_len, kvc_past, kvs_past, kvw_buf, keep, w_in, qk_gain, cmp_pe, cmp_w1, cmp_w2, w_out):
    b, t = h.shape[0], h.shape[1]
    proj = h @ w_in
    q, kvc, kvs, kvw, gate = jnp.split(
        proj, [NSA_Q_DIM, NSA_Q_DIM + NSA_KV_DIM, NSA_Q_DIM + 2 * NSA_KV_DIM, NSA_Q_DIM + 3 * NSA_KV_DIM], axis=-1)
    kv_shape = (b, t, 2, NSA_KV_GROUPS, NSA_HEAD_DIM)
    q = rms_norm(q.reshape(b, t, NSA_HEADS, NSA_HEAD_DIM), qk_gain[0])
    kvc = kvc.reshape(kv_shape)
    kvs = kvs.reshape(kv_shape)
    kvs = jnp.stack([rms_norm(kvs[:, :, 0], qk_gain[2]), kvs[:, :, 1]], axis=2)
    kvw = kvw.reshape(kv_shape)
    kvw = jnp.stack([rms_norm(kvw[:, :, 0], qk_gain[3]), kvw[:, :, 1]], axis=2)
    gate = jax.nn.sigmoid(gate.astype(jnp.float32)).reshape(b, t, 3, NSA_HEADS)
    full_c = jnp.concatenate([kvc_past.astype(h.dtype), kvc], axis=1)
    full_s = jnp.concatenate([kvs_past.astype(h.dtype), kvs], axis=1)
    win = jnp.concatenate([kvw_buf.astype(h.dtype), kvw], axis=1)
    kc = rms_norm(compress_blocks(full_c[:, :, 0], cmp_pe[0], cmp_w1[0], cmp_w2[0]), qk_gain[1])
    vc = compress_blocks(full_c[:, :, 1], cmp_pe[1], cmp_w1[1], cmp_w2[1])
    q_pos = past_len + jnp.arange(t, dtype=jnp.int32)
    buf = kvw_buf.shape[1]
    w_pos = (past_len - buf) + jnp.arange(buf + t, dtype=jnp.int32)
    o_c, o_s, o_w = nsa_attend(q, q_pos, kc, vc, full_s[:, :, 0], full_s[:, :, 1], win[:, :, 0], win[:, :, 1], w_pos)
    o = gate[:, :, 0, :, None] * o_c + gate[:, :, 1, :, None] * o_s + gate[:, :, 2, :, None] * o_w
    y = o.astype(h.dtype).reshape(b, t, NSA_Q_DIM) @ w_out
    return y, kvc, kvs, win[:, win.shape[1] - keep:]

def ssd_scan(x, dt, a, bm, cm, h0):
    b, t = x.shape[0], x.shape[1]
    f32 = jnp.float32
    lc = SSM_CHUNK if t % SSM_CHUNK == 0 else t
    nc = t // lc

    def chunked(v, tail):
        return jnp.moveaxis(v.astype(f32).reshape((b, nc, lc) + tail), 1, 0)

    xs = chunked(x, (SSM_GROUPS, SSM_HEADS_PER_GROUP, SSM_HEAD_DIM))
    dts = chunked(dt, (SSM_GROUPS, SSM_HEADS_PER_GROUP))
    bs = chunked(bm, (SSM_GROUPS, SSM_STATE))
    cs = chunked(cm, (SSM_GROUPS, SSM_STATE))
    a_g = a.astype(f32).reshape(SSM_GROUPS, SSM_HEADS_PER_GROUP)
    causal = jnp.tril(jnp.ones((lc, lc), dtype=bool))[None, :, :, None, None]

    def step(h_prev, inp):
        xc, dtc, bc, cc = inp
        acum = jnp.cumsum(dtc * a_g, axis=1)
        seg = acum[:, :, None] - acum[:, None, :]
        decay = jnp.exp(jnp.where(causal, seg, -jnp.inf))
        cb = jnp.einsum("blgn,bsgn->blsg", cc, bc)
        xdt = xc * dtc[..., None]
        y = (jnp.einsum("blsgr,bsgrp->blgrp", cb[..., None] * decay, xdt)
             + jnp.einsum("blgn,bgrpn->blgrp", cc, h_prev) * jnp.exp(acum)[..., None])
        to_end = jnp.exp(acum[:, -1:] - acum)
        h_new = (h_prev * jnp.exp(acum[:, -1])[..., None, None]
                 + jnp.einsum("bsgn,bsgrp->bgrpn", bc, xdt * to_end[..., None]))
        return h_new, y

    h0g = h0.astype(f32).reshape(b, SSM_GROUPS, SSM_HEADS_PER_GROUP, SSM_HEAD_DIM, SSM_STATE)
    h_last, ys = lax.scan(step, h0g, (xs, dts, bs, cs))
    y = jnp.moveaxis(ys, 0, 1).reshape(b, t, SSM_HEADS, SSM_HEAD_DIM)
    return y, h_last.reshape(b, SSM_HEADS, SSM_HEAD_DIM, SSM_STATE)

def ssd_layer(h, conv_state, ssm_state, w_in, conv_w, conv_b, dt_bias, a_log, d_skip, norm_w, w_out):
    b, t = h.shape[0], h.shape[1]
    proj = h @ w_in
    z, xbc, dt_raw = jnp.split(proj, [SSM_D_INNER, SSM_D_INNER + SSM_CONV_DIM], axis=-1)
    xbc_full = jnp.concatenate([conv_state.astype(h.dtype), xbc], axis=1)
    conv = conv_b
    for k in range(SSM_CONV):
        conv = conv + xbc_full[:, k:k + t] * conv_w[k]
    conv = jax.nn.silu(conv)
    xh, bm, cm = jnp.split(conv, [SSM_D_INNER, SSM_D_INNER + SSM_GROUPS * SSM_STATE], axis=-1)
    xh = xh.reshape(b, t, SSM_HEADS, SSM_HEAD_DIM)
    bm = bm.reshape(b, t, SSM_GROUPS, SSM_STATE)
    cm = cm.reshape(b, t, SSM_GROUPS, SSM_STATE)
    dt = jax.nn.softplus(dt_raw.astype(jnp.float32) + dt_bias.astype(jnp.float32))
    a = -jnp.exp(a_log.astype(jnp.float32))
    y, h_last = ssd_scan(xh, dt, a, bm, cm, ssm_state)
    y = y + xh.astype(jnp.float32) * d_skip.astype(jnp.float32)[:, None]
    gated = y.reshape(b, t, SSM_D_INNER) * jax.nn.silu(z.astype(jnp.float32))
    gated = rms_norm(gated.reshape(b, t, SSM_GROUPS, SSM_D_INNER // SSM_GROUPS),
                     norm_w.reshape(SSM_GROUPS, SSM_D_INNER // SSM_GROUPS)).reshape(b, t, SSM_D_INNER)
    out = gated.astype(h.dtype) @ w_out
    return out, xbc_full[:, xbc_full.shape[1] - (SSM_CONV - 1):], h_last.astype(ssm_state.dtype)

def setup_inputs(seed: int = 0) -> dict:
    key = jax.random.key(seed)
    ks = jax.random.split(key, 32)
    f32 = jnp.float32
    nrm = jax.random.normal
    n_pages = PAST_LEN // PAGE_SIZE
    n_used = DEC_BATCH * n_pages
    n_phys = n_used + -(-n_used // 4)
    win_rows = min(WINDOW, PAST_LEN)
    kvp = (2, NSA_KV_GROUPS, NSA_HEAD_DIM)

    def gain(k, shape):
        return 1.0 + 0.02 * nrm(k, shape, f32)

    x_prompt = nrm(ks[0], (BATCH, SEQ, D_MODEL), f32)
    x_sample = nrm(ks[1], (DEC_BATCH, DEC_SEQ, D_MODEL), f32)
    cache_kv_cmp = nrm(ks[2], (N_NSA_LAYERS, n_phys, PAGE_SIZE) + kvp, f32)
    cache_kv_sel = nrm(ks[3], (N_NSA_LAYERS, n_phys, PAGE_SIZE) + kvp, f32)
    cache_kv_win = nrm(ks[4], (N_NSA_LAYERS, DEC_BATCH, win_rows) + kvp, f32)
    state_conv = nrm(ks[5], (N_SSD_LAYERS, DEC_BATCH, SSM_CONV - 1, SSM_CONV_DIM), f32)
    state_ssm = 0.1 * nrm(ks[6], (N_SSD_LAYERS, DEC_BATCH, SSM_HEADS, SSM_HEAD_DIM, SSM_STATE), f32)
    page_table = jax.random.permutation(ks[7], n_phys)[:n_used].reshape(DEC_BATCH, n_pages).astype(jnp.int32)

    norm_mix = gain(ks[8], (DEPTH, D_MODEL))
    norm_ffn = gain(ks[9], (DEPTH, D_MODEL))
    nsa_w_in = nrm(ks[10], (N_NSA_LAYERS, D_MODEL, NSA_IN), f32) * D_MODEL ** -0.5
    nsa_qk_gain = gain(ks[11], (N_NSA_LAYERS, 4, NSA_HEAD_DIM))
    nsa_cmp_pe = 0.1 * nrm(ks[12], (N_NSA_LAYERS, 2, CMP_BLOCK, NSA_HEAD_DIM), f32)
    nsa_cmp_w1 = nrm(ks[13], (N_NSA_LAYERS, 2, CMP_BLOCK, NSA_HEAD_DIM, CMP_HIDDEN), f32) * (CMP_BLOCK * NSA_HEAD_DIM) ** -0.5
    nsa_cmp_w2 = nrm(ks[14], (N_NSA_LAYERS, 2, CMP_HIDDEN, NSA_HEAD_DIM), f32) * CMP_HIDDEN ** -0.5
    nsa_w_out = nrm(ks[15], (N_NSA_LAYERS, NSA_Q_DIM, D_MODEL), f32) * NSA_Q_DIM ** -0.5

    ssd_w_in = nrm(ks[16], (N_SSD_LAYERS, D_MODEL, SSM_IN), f32) * D_MODEL ** -0.5
    ssd_conv_w = nrm(ks[17], (N_SSD_LAYERS, SSM_CONV, SSM_CONV_DIM), f32) * SSM_CONV ** -0.5
    ssd_conv_b = 0.01 * nrm(ks[18], (N_SSD_LAYERS, SSM_CONV_DIM), f32)
    dt0 = jnp.exp(jax.random.uniform(ks[19], (N_SSD_LAYERS, SSM_HEADS), f32, math.log(1e-3), math.log(1e-1)))
    ssd_dt_bias = dt0 + jnp.log(-jnp.expm1(-dt0))
    ssd_a_log = jnp.log(jax.random.uniform(ks[20], (N_SSD_LAYERS, SSM_HEADS), f32, 1.0, 16.0))
    ssd_d = gain(ks[21], (N_SSD_LAYERS, SSM_HEADS))
    ssd_norm = gain(ks[22], (N_SSD_LAYERS, SSM_D_INNER))
    ssd_w_out = nrm(ks[23], (N_SSD_LAYERS, SSM_D_INNER, D_MODEL), f32) * SSM_D_INNER ** -0.5

    ffn_w_gate = nrm(ks[24], (DEPTH, D_MODEL, FFN_HIDDEN), f32) * D_MODEL ** -0.5
    ffn_w_up = nrm(ks[25], (DEPTH, D_MODEL, FFN_HIDDEN), f32) * D_MODEL ** -0.5
    ffn_w_down = nrm(ks[26], (DEPTH, FFN_HIDDEN, D_MODEL), f32) * FFN_HIDDEN ** -0.5

    return {
        "x_prompt": x_prompt, "x_sample": x_sample,
        "cache_kv_cmp": cache_kv_cmp, "cache_kv_sel": cache_kv_sel, "cache_kv_win": cache_kv_win,
        "state_conv": state_conv, "state_ssm": state_ssm, "page_table": page_table,
        "norm_mix": norm_mix, "norm_ffn": norm_ffn,
        "nsa_w_in": nsa_w_in, "nsa_qk_gain": nsa_qk_gain, "nsa_cmp_pe": nsa_cmp_pe,
        "nsa_cmp_w1": nsa_cmp_w1, "nsa_cmp_w2": nsa_cmp_w2, "nsa_w_out": nsa_w_out,
        "ssd_w_in": ssd_w_in, "ssd_conv_w": ssd_conv_w, "ssd_conv_b": ssd_conv_b,
        "ssd_dt_bias": ssd_dt_bias, "ssd_a_log": ssd_a_log, "ssd_d": ssd_d,
        "ssd_norm": ssd_norm, "ssd_w_out": ssd_w_out,
        "ffn_w_gate": ffn_w_gate, "ffn_w_up": ffn_w_up, "ffn_w_down": ffn_w_down,
    }

def reference(x_prompt, x_sample, cache_kv_cmp, cache_kv_sel, cache_kv_win, state_conv, state_ssm, page_table,
              norm_mix, norm_ffn, nsa_w_in, nsa_qk_gain, nsa_cmp_pe, nsa_cmp_w1, nsa_cmp_w2, nsa_w_out,
              ssd_w_in, ssd_conv_w, ssd_conv_b, ssd_dt_bias, ssd_a_log, ssd_d, ssd_norm, ssd_w_out,
              ffn_w_gate, ffn_w_up, ffn_w_down):
    xp, xs = x_prompt, x_sample
    bp, tp = xp.shape[0], xp.shape[1]
    past_len = page_table.shape[1] * PAGE_SIZE
    kvp = (2, NSA_KV_GROUPS, NSA_HEAD_DIM)
    cmp_p, sel_p, win_p, conv_p, ssm_p = [], [], [], [], []
    cmp_s, sel_s, win_s, conv_s, ssm_s = [], [], [], [], []
    for i in range(DEPTH):
        l = i // N_MIXERS
        hp = rms_norm(xp, norm_mix[i])
        hs = rms_norm(xs, norm_mix[i])
        if i % N_MIXERS == 0:
            w = (nsa_w_in[l], nsa_qk_gain[l], nsa_cmp_pe[l], nsa_cmp_w1[l], nsa_cmp_w2[l], nsa_w_out[l])
            empty = jnp.zeros((bp, 0) + kvp, xp.dtype)
            yp, c_new, s_new, w_new = nsa_layer(hp, 0, empty, empty, jnp.zeros((bp, WINDOW) + kvp, xp.dtype),
                                                min(WINDOW, tp), *w)
            cmp_p.append(c_new)
            sel_p.append(s_new)
            win_p.append(w_new)
            past_c = gather_pages(cache_kv_cmp[l], page_table)
            past_s = gather_pages(cache_kv_sel[l], page_table)
            y_s, c_new, s_new, w_new = nsa_layer(hs, past_len, past_c, past_s, cache_kv_win[l],
                                                 cache_kv_win.shape[2], *w)
            cmp_s.append(c_new)
            sel_s.append(s_new)
            win_s.append(w_new)
        else:
            w = (ssd_w_in[l], ssd_conv_w[l], ssd_conv_b[l], ssd_dt_bias[l], ssd_a_log[l], ssd_d[l],
                 ssd_norm[l], ssd_w_out[l])
            yp, cv_new, st_new = ssd_layer(hp, jnp.zeros((bp, SSM_CONV - 1, SSM_CONV_DIM), xp.dtype),
                                           jnp.zeros((bp, SSM_HEADS, SSM_HEAD_DIM, SSM_STATE), xp.dtype), *w)
            conv_p.append(cv_new)
            ssm_p.append(st_new)
            y_s, cv_new, st_new = ssd_layer(hs, state_conv[l], state_ssm[l], *w)
            conv_s.append(cv_new)
            ssm_s.append(st_new)
        xp = xp + yp
        xs = xs + y_s
        xp = xp + swiglu(rms_norm(xp, norm_ffn[i]), ffn_w_gate[i], ffn_w_up[i], ffn_w_down[i])
        xs = xs + swiglu(rms_norm(xs, norm_ffn[i]), ffn_w_gate[i], ffn_w_up[i], ffn_w_down[i])
    return (xp, xs,
            jnp.stack(cmp_p), jnp.stack(sel_p), jnp.stack(win_p), jnp.stack(conv_p), jnp.stack(ssm_p),
            jnp.stack(cmp_s), jnp.stack(sel_s), jnp.stack(win_s), jnp.stack(conv_s), jnp.stack(ssm_s))


_drawn_inputs = setup_inputs


def setup_inputs(seed=0):
    import zlib

    import numpy as np

    out = dict(_drawn_inputs(seed))
    spreads = {}
    factors = {'nsa_qk_gain': 3.989,
     'ssd_conv_b': 3.456,
     'ssd_d': 42.63,
     'ssd_norm': 12.323,
     'norm_ffn': 2.823}
    for name, (base, spread) in spreads.items():
        noise = np.random.default_rng([zlib.crc32(name.encode()), seed]).standard_normal(out[name].shape)
        drawn = base * np.exp(spread * noise) if base else spread * noise
        out[name] = jnp.asarray(drawn.astype(out[name].dtype))
    for name, factor in factors.items():
        out[name] = (out[name] * factor).astype(out[name].dtype)
    return out
```

```python
from contextlib import ExitStack

import numpy as np

import concourse.bass as bass
from concourse import mybir

F32 = mybir.dt.float32
I32 = mybir.dt.int32
ALU = mybir.AluOpType
ACT = mybir.ActivationFunctionType
AX = mybir.AxisListType

P = 128
D = 1024
KT = D // P
SEQ = 512
NB = 8
TS = 4
NS = NB * TS
NT = SEQ + NS
HALF = NT // 2
PAST = 2048
PAGE = 128
NPAGE = PAST // PAGE
NPHYS = NB * NPAGE + NB * NPAGE // 4
HEADS = 16
HD = 64
GROUPS = 4
QT = 4
CW = 16
CHUNKS = PAST // CW
NC = CHUNKS - 1
PCH = SEQ // CW
NCP = PCH - 1
SELB = 64
NBLK = PAST // SELB
FREE_BLOCKS = NBLK - 2
TAKE = 16 - 3
HID = 2816
FT = HID // P
SI = 2048
ST = SI // P
CT = 24
SH = 32
RAW = SEQ + 3 + NB * (TS + 3)
CONV = RAW - 3
EPS = 1e-6
NEG = -1e30
SLOT = 2048
RING = 4
PAIRS = NB // 2


def slopes():
    return (np.float64(2.0 ** (-8.0 / HEADS)) ** np.arange(1, HEADS + 1)).astype(np.float32)


def head_of(kt, a):
    return (2 * (kt // 4) + a) * 4 + kt % 4


def row_head(row):
    gp, a, r = row // 32 % 2, row // 16 % 2, row // 4 % 4
    return (2 * gp + a) * 4 + r


def columns(widths):
    at, out = 0, {}
    for name, w in widths:
        out[name] = slice(at, at + w)
        at += w
    return out, at


CONST_A, NA = columns([("ident", P), ("ones", P), ("window", 70), ("onecol", 7), ("eps", 1), ("qscale", KT)])
CONST_N, NN = columns([("same_gt", P), ("dist", SEQ), ("dist_c", QT * NCP), ("seen_c", QT * NCP),
                       ("slope_c", HEADS * NCP), ("ali_c", NC), ("tail", PAIRS * NS), ("ali_w", SEQ),
                       ("lower", FREE_BLOCKS * FREE_BLOCKS), ("own_head", HEADS), ("row_of", PAIRS * P)])
CONST_S, NSC = columns([("causal", P), ("causal_s", NS), ("keep", NT), ("own", NB)])


def const_a():
    c = np.zeros((P, NA), np.float32)
    p = np.arange(P)
    c[:, CONST_A["ident"]] = np.eye(P)
    c[:, CONST_A["ones"]] = 1
    w = c[:, CONST_A["window"]]
    w[p, 34 + p // HD] = 1
    c[:, CONST_A["onecol"]][:, 3] = 1
    c[:, CONST_A["eps"]] = EPS
    s = slopes()
    for kt in range(KT):
        for a in range(2):
            c[a * HD:(a + 1) * HD, CONST_A["qscale"]][:, kt] = np.float32(HD ** -0.5) / s[head_of(kt, a)]
    return c


def const_n():
    c = np.zeros((P, NN), np.float32)
    s, row = slopes(), np.arange(P)
    seq, t = row // HD, row % 4
    rs = s[[row_head(x) for x in row]][:, None]
    c[:, CONST_N["same_gt"]] = (row[:, None] // 16 == row[None] // 16) & (t[:, None] == t[None])
    d = np.arange(SEQ)[None] - (SEQ - P) - row[:, None]
    c[:, CONST_N["dist"]] = np.where(d <= 0, d, NEG)
    pos = np.arange(QT)[None, :, None] * P + row[:, None, None]
    d = np.arange(NCP)[None, None] * CW + 2 * CW - 1 - pos
    c[:, CONST_N["dist_c"]] = np.where(d <= 0, d, NEG).reshape(P, -1)
    c[:, CONST_N["seen_c"]] = (d <= 0).reshape(P, -1)
    order = [head_of(i // 2, i % 2) for i in range(HEADS)]
    c[:, CONST_N["slope_c"]] = np.repeat(s[order], NCP)[None]
    tq = PAST + t[:, None]
    c[:, CONST_N["ali_c"]] = rs * (np.arange(NC)[None] * CW + 2 * CW - 1 - tq)
    new = np.arange(NS)[None]
    for pr in range(PAIRS):
        ok = (new // TS == 2 * pr + seq[:, None]) & (new % TS <= t[:, None])
        c[:, CONST_N["tail"]][:, pr * NS:(pr + 1) * NS] = np.where(ok, rs * (new % TS - t[:, None]), NEG)
    key = PAST - SEQ + np.arange(SEQ)[None]
    c[:, CONST_N["ali_w"]] = np.where(tq - key < SEQ, rs * (key - tq), NEG)
    b = np.arange(FREE_BLOCKS)
    c[:, CONST_N["lower"]] = (b[None] < b[:, None]).reshape(1, -1)
    for pr in range(PAIRS):
        tok = (2 * pr + seq) * TS + t
        c[:, CONST_N["row_of"]][:, pr * P:(pr + 1) * P] = tok[None] == row[:, None]
    c[:, CONST_N["own_head"]] = np.arange(HEADS)[None] == np.array([row_head(x) for x in row])[:, None]
    return c


def const_ali():
    row = np.arange(P)
    rs = slopes()[[row_head(x) for x in row]][:, None]
    return (rs * (np.arange(PAST)[None] - (PAST + row % 4)[:, None])).astype(np.float32)


def const_s():
    c = np.zeros((P, NSC), np.float32)
    i = np.arange(P)
    c[:, CONST_S["causal"]] = np.where(i[None] >= i[:, None], 0, NEG)
    j = np.arange(NS)
    ok = (j[None] // TS == i[:, None] // TS) & (j[None] >= i[:, None])
    c[:, CONST_S["causal_s"]] = np.where(ok, 0, NEG)
    tok = np.arange(NT)
    c[:, CONST_S["keep"]] = np.where(tok < SEQ, tok % P != 0, tok % TS != 0)[None]
    c[:, CONST_S["own"]] = np.arange(NB)[None] == i[:, None] // TS
    return c


PAR, NPAR = columns([("g_mix", 2 * KT), ("g_ffn", 2 * KT), ("qk", 4), ("pe", 2 * 2 * KT), ("w2", 2 * 2 * HD),
                     ("w_gate", KT * 48), ("w_dt", KT * SH), ("conv_w", CT * 4), ("conv_b", CT), ("d_skip", ST),
                     ("ssm_norm", ST), ("a_log", 1), ("dt_bias", 1), ("conv_state", CT * NB * 3)])


class InOrder:

    def __init__(self, eng, own):
        self.eng, self.own, self.count = eng, own, {}

    def __call__(self, ins, signal=None):
        s = signal or self.own
        self.count[s.name] = self.count.get(s.name, 0) + 1
        ins.then_inc(s, 1)
        self.eng.wait_ge(s, self.count[s.name])


def build(nc, t):
    ctx = ExitStack()
    with ctx:
        arena = ctx.enter_context(nc.sbuf_tensor("sbuf", [P, 52900], F32))
        pages = ctx.enter_context(nc.sbuf_tensor("page_numbers", [1, NB * NPAGE], I32))
        ps = ctx.enter_context(nc.psum_tensor("ps", [P, 8, 512], F32))

        names = set()

        def sem(name):
            assert name not in names
            names.add(name)
            return ctx.enter_context(nc.semaphore(name))

        top = [0]

        def region(n):
            at = top[0]
            top[0] += n
            assert top[0] <= 52900, top[0]
            return arena[:, at:at + n]

        xT = region(KT * NT).rearrange("p (k n) -> p k n", k=KT)
        ring = region(RING * SLOT).rearrange("p (s n) -> p s n", s=RING)
        hT = region(KT * NT).rearrange("p (k n) -> p k n", k=KT)
        rstd = region(NT)
        par = region(NPAR)
        ca = region(NA)
        phase_base = top[0]
        ident = ca[:, CONST_A["ident"]]
        ones = ca[:, CONST_A["ones"]]
        window = ca[:, CONST_A["window"]]
        onecol = ca[:, CONST_A["onecol"]]
        eps = ca[:, CONST_A["eps"]]
        hT_flat = hT.rearrange("p k n -> p (k n)")

        qT = region(KT * NT).rearrange("p (k n) -> p k n", k=KT)
        kvT_flat = region(12 * NT)
        kvT = kvT_flat.rearrange("p (k n) -> p k n", k=12)
        KV_TILE = {"kc": 0, "vc": 2, "vs": 4, "vw": 6, "ks": 8, "kw": 10}
        kcT = region(NB * 2 * NC).rearrange("p (b g n) -> p b g n", b=NB, g=2)
        kcP = region(2 * NCP).rearrange("p (g n) -> p g n", g=2)
        vcS = region(NB * 256).rearrange("p (b n) -> p b n", b=NB)
        vcP = region(256)
        gates = region(5 * 48).rearrange("p (i c) -> p i c", i=5)
        gate_rows = region(PAIRS * 3).rearrange("p (i c) -> p i c", i=PAIRS)
        vnew = region(2 * 256).rearrange("p (b n) -> p b n", b=2)
        att_base = top[0]

        met = sem("phase_met")
        x_in, par_in, ca_in, cn_in, ali_in, cs_in, pages_in = [
            sem(n) for n in ("x_in", "par_in", "ca_in", "cn_in", "ali_in", "cs_in", "pages_in")]
        w_in = [sem(f"slot{i}_in") for i in range(RING)]
        w_used = sem("slots_used")
        act_own, dve_own, pool_own = sem("act_order"), sem("dve_order"), sem("pool_order")
        stored = sem("stored")

        block = ctx.enter_context(nc.Block())
        PE, ACTE, DVE, POOL, SP = [], [], [], [], []


        def meet(eng, k):
            eng.drain().then_inc(met, 1)
            eng.wait_ge(met, 4 * k)

        slot_at = {}
        at = 0
        for name, n in (("nsa_in", 10), ("w1", 4), ("nsa_out", 4), ("gu0", FT), ("down0", 16),
                        ("ssd_in", 20), ("ssd_out", 8), ("gu1", FT), ("down1", 16)):
            slot_at[name] = at
            at += n

        def slot_wait(eng, s):
            eng.wait_ge(w_in[s % RING], 16 * (s // RING + 1))

        def stationary(s, tile, kt, kts=KT):
            o = (tile * kts + kt) * P
            return ring[:, s % RING, o:o + P]

        def load_slots(sp, name, src, n, width=SLOT):
            s0 = slot_at[name]
            for i in range(n):
                s = s0 + i
                if s >= RING:
                    sp.wait_ge(w_used, s - RING + 1)
                sp.dma_start(ring[:, s % RING, 0:width], src[i]).then_inc(w_in[s % RING], 16)

        def pair_ap(q):
            return ps[:, 2 * q:2 * q + 2, 0:HALF]

        def halves(ap):
            return ap.rearrange("p (h n) -> p h n", h=2)

        def dense(pe, s, tile, q, rhs, kts=KT, kt0=0, kt_all=None):
            kt_all = kt_all or kts
            for kt in range(kts):
                for h in range(2):
                    last = pe.matmul(ps[:, 2 * q + h, 0:HALF], stationary(s, tile, kt, kts),
                                     rhs[:, kt0 + kt, h * HALF:(h + 1) * HALF],
                                     start=kt0 + kt == 0, stop=kt0 + kt == kt_all - 1)
            return last

        n_scaled, n_sq, n_ss, n_rt, n_r = [sem(f"norm_{n}") for n in ("scaled", "squared", "summed", "root", "rstd")]

        class Norm:

            def __init__(self, i, roots, gain, squares, residual=None, seen=0):
                self.residual, self.seen = residual, seen
                self.tiles, self.roots = i * KT, roots
                self.gain, self.squares = gain, squares

            def wait_scaled(self, eng):
                eng.wait_ge(n_scaled, self.tiles + KT)

            def wait_root(self, eng):
                eng.wait_ge(n_rt, self.roots + 1)

            def dve(self, dve, do):
                for kt in range(KT):
                    do(dve.tensor_scalar(hT[:, kt], xT[:, kt], par[:, self.gain + kt:self.gain + kt + 1],
                                         None, ALU.mult), n_scaled)
                self.wait_root(dve)
                do(dve.reciprocal(rstd, rstd), n_r)

            def act(self, act, do):
                for kt in range(KT):
                    if self.residual:
                        act.wait_ge(self.residual, self.seen + kt + 1)
                    do(act.activation(self.squares[:, kt], xT[:, kt], ACT.Square), n_sq)
                act.wait_ge(n_ss, self.roots + 1)
                do(act.activation(halves(rstd), pair_ap(0), ACT.Sqrt, bias=eps, scale=1.0 / D), n_rt)

            def pe(self, pe):
                if self.residual:
                    pe.wait_ge(self.residual, self.seen + KT)
                for kt in range(KT):
                    pe.wait_ge(n_sq, self.tiles + kt + 1)
                    for h in range(2):
                        last = pe.matmul(ps[:, h, 0:HALF], ones, self.squares[:, kt, h * HALF:(h + 1) * HALF],
                                         start=kt == 0, stop=kt == KT - 1)
                last.then_inc(n_ss, 1)

        top[0] = att_base
        sq1 = region(KT * NT).rearrange("p (k n) -> p k n", k=KT)
        top[0] = att_base + 8192
        nsq = region(12 * NT).rearrange("p (k n) -> p k n", k=12)
        q_gain = region(KT + 1)
        rq = region(NT)
        rcol = region(8)
        head_pick = region(3 * HEADS).rearrange("p (b h) -> p b h", b=3)
        cn_early = region(HEADS + PAIRS * P)
        norm1 = Norm(0, 0, PAR["g_mix"].start, sq1)
        in_ev = sem("in_taken")
        hs_sq, hs_ss, hs_rt, hs_r, hs_bc, hs_out = [sem(f"qk_{n}") for n in
                                                     ("squared", "summed", "root", "rstd", "spread", "normed")]
        g_mm, g_col, g_neg, g_exp, g_rows, g_done = [sem(f"gate_{n}") for n in
                                                     ("product", "col", "neg", "exp", "rows", "done")]
        NORMED = [("q", kt) for kt in range(KT)] + [("ks", 0), ("ks", 1), ("kw", 0), ("kw", 1)]
        TILE_DST = [("q", kt) for kt in range(KT)] + [(n, i) for n in ("kc", "vc", "ks", "vs", "kw", "vw")
                                                      for i in range(2)]

        def tile_of(name, i):
            return qT[:, i] if name == "q" else kvT[:, KV_TILE[name] + i]

        def p1_sp(sp):
            sp.dma_start(xT, t["x"]).then_inc(x_in, 16)
            sp.dma_start(par, t["par"]).then_inc(par_in, 16)
            sp.dma_start(ca, t["const_a"]).then_inc(ca_in, 16)
            load_slots(sp, "nsa_in", t["w_nsa_in"], 4)
            sp.dma_start(pages[:], t["pages"]).then_inc(pages_in, 16)
            sp.dma_start(cn_early, t["const_n"][:, CONST_N["own_head"].start:NN]).then_inc(cn_in, 16)
            s0 = slot_at["nsa_in"]
            for i in range(4, 10):
                sp.wait_ge(w_used, i - RING + 1)
                sp.dma_start(ring[:, i % RING], t["w_nsa_in"][i]).then_inc(w_in[i % RING], 16)
        SP.append(p1_sp)

        def p1_pe(pe):
            pe.wait_ge(ca_in, 16)
            norm1.pe(pe)
            for m in range(20):
                s = slot_at["nsa_in"] + m // 2
                if m % 2 == 0:
                    slot_wait(pe, s)
                if m == 0:
                    pe.wait_ge(n_scaled, KT)
                if m == 3:
                    pe.wait_ge(n_rt, 1)
                if m >= 4:
                    pe.wait_ge(in_ev, m - 3)
                last = dense(pe, s, m % 2, (m + 1) % 4, hT)
                if m % 2 == 1:
                    last.then_inc(w_used, 1)
            pe.wait_ge(in_ev, 20)
            for j in range(12):
                pe.wait_ge(hs_sq, j + 1)
                for h in range(2):
                    last = pe.matmul(ps[0:24, h, 0:HALF], window[:, 34 - 2 * j:58 - 2 * j],
                                     nsq[:, j, h * HALF:(h + 1) * HALF], start=j == 0, stop=j == 11)
            last.then_inc(hs_ss, 1)
            pe.wait_ge(n_r, 1)
            pe.wait_ge(par_in, 16)
            for i in range(5):
                o, n = i * P, P if i < QT else NS
                last = pe.matmul(ps[0:n, 2, i:i + 1], rstd[0:1, o:o + n], ones[0:1, 0:1], start=True, stop=True)
            last.then_inc(g_col, 1)
            wg = par[:, PAR["w_gate"]].rearrange("p (k c) -> p k c", k=KT)
            for i in range(5):
                o, n = i * P, P if i < QT else NS
                for kt in range(KT):
                    last = pe.matmul(ps[0:n, 3, i * 48:(i + 1) * 48], hT[:, kt, o:o + n], wg[:, kt],
                                     start=kt == 0, stop=kt == KT - 1)
            last.then_inc(g_mm, 1)
            pe.wait_ge(hs_r, 1)
            for j in range(12):
                if j >= 2:
                    pe.wait_ge(hs_out, j - 1)
                for h in range(2):
                    for a in range(2):
                        last = pe.matmul(ps[a * HD:(a + 1) * HD, 4 + 2 * (j % 2) + h, 0:HALF],
                                         ident[0:24, 2 * j + a:2 * j + a + 1].to_broadcast([24, HD]),
                                         rq[0:24, h * HALF:(h + 1) * HALF], start=True, stop=True)
                last.then_inc(hs_bc, 1)
            pe.wait_ge(g_done, 1)
            pe.wait_ge(cn_in, 16)
            for pr in range(PAIRS):
                last = pe.matmul(ps[:, 2, 64 + pr * 48:64 + (pr + 1) * 48],
                                 cn_early[0:NS, HEADS + pr * P:HEADS + (pr + 1) * P], gates[0:NS, QT],
                                 start=True, stop=True)
            last.then_inc(g_rows, 1)
            meet(pe, 1)
        PE.append(p1_pe)

        def p1_act(act):
            do = act_do
            act.wait_ge(x_in, 16)
            act.wait_ge(ca_in, 16)
            norm1.act(act, do)
            for j, (name, i) in enumerate(NORMED):
                m = TILE_DST.index((name, i))
                act.wait_ge(in_ev, m + 1)
                do(act.activation(nsq[:, j], tile_of(name, i), ACT.Square), hs_sq)
            act.wait_ge(hs_ss, 1)
            do(act.activation(halves(rq)[0:24], ps[0:24, 0:2, 0:HALF], ACT.Sqrt, bias=eps[0:24], scale=1.0 / HD), hs_rt)
            act.wait_ge(g_mm, 1)
            act.wait_ge(g_neg, 1)
            for i in range(5):
                n = P if i < QT else NS
                do(act.activation(gates[0:n, i], ps[0:n, 3, i * 48:(i + 1) * 48], ACT.Exp, scale=rcol[0:n, i:i + 1]),
                   g_exp)
            meet(act, 1)
        ACTE.append(p1_act)

        def p1_dve(dve):
            do = dve_do
            dve.wait_ge(x_in, 16)
            dve.wait_ge(par_in, 16)
            norm1.dve(dve, do)
            dve.wait_ge(ca_in, 16)
            qk = par[:, PAR["qk"]]
            do(dve.tensor_scalar(q_gain[:, 0:KT], ca[:, CONST_A["qscale"]], qk[:, 0:1], None, ALU.mult))
            do(dve.tensor_scalar(q_gain[:, KT:KT + 1], qk[:, 0:1], HD ** -0.5, None, ALU.mult))
            for m, (name, i) in enumerate(TILE_DST):
                dve.wait_ge(w_used, slot_at["nsa_in"] + m // 2 + 1)
                do(dve.tensor_tensor(halves(tile_of(name, i)), pair_ap((m + 1) % 4), halves(rstd), ALU.mult), in_ev)
            dve.wait_ge(g_col, 1)
            do(dve.tensor_scalar(rcol[:, 0:QT], ps[:, 2, 0:QT], -1.0, None, ALU.mult))
            do(dve.tensor_scalar(rcol[0:NS, QT:QT + 1], ps[0:NS, 2, QT:QT + 1], -1.0, None, ALU.mult), g_neg)
            dve.wait_ge(hs_rt, 1)
            do(dve.reciprocal(rq[0:24], rq[0:24]), hs_r)
            for j, (name, i) in enumerate(NORMED):
                dve.wait_ge(hs_bc, j + 1)
                q, dst = 2 + j % 2, tile_of(name, i)
                b0, b1 = ps[:, 2 * q, 0:HALF], ps[:, 2 * q + 1, 0:HALF]
                if name == "q":
                    g = q_gain[:, i:i + 1]
                    do(dve.scalar_tensor_tensor(dst[:, 0:HALF], dst[:, 0:HALF], g, b0, ALU.mult, ALU.mult))
                    do(dve.scalar_tensor_tensor(dst[:, HALF:SEQ], dst[:, HALF:SEQ], g, b1[:, 0:SEQ - HALF],
                                                ALU.mult, ALU.mult))
                    do(dve.scalar_tensor_tensor(dst[:, SEQ:NT], dst[:, SEQ:NT], q_gain[:, KT:KT + 1],
                                                b1[:, SEQ - HALF:HALF], ALU.mult, ALU.mult), hs_out)
                else:
                    g = qk[:, 2:3] if name == "ks" else qk[:, 3:4]
                    do(dve.scalar_tensor_tensor(halves(dst), halves(dst), g, pair_ap(q), ALU.mult, ALU.mult), hs_out)
            dve.wait_ge(g_exp, 5)
            for ap, signal in ((gates[:, 0:QT].rearrange("p i c -> p (i c)"), None), (gates[0:NS, QT], g_done)):
                do(dve.tensor_scalar(ap, ap, 1.0, None, ALU.add))
                do(dve.reciprocal(ap, ap), signal)
            dve.wait_ge(g_rows, 1)
            for pr in range(PAIRS):
                do(dve.tensor_tensor(head_pick, ps[:, 2, 64 + pr * 48:64 + (pr + 1) * 48].rearrange(
                    "p (b h) -> p b h", b=3), cn_early[:, 0:HEADS].unsqueeze(1).to_broadcast([P, 3, HEADS]), ALU.mult))
                do(dve.tensor_reduce(gate_rows[:, pr], head_pick, AX.X, ALU.add))
            meet(dve, 1)
        DVE.append(p1_dve)

        def p1_pool(pool):
            meet(pool, 1)
            pool.dma_start(t["out_kv"], kvT).then_inc(stored, 16)
        POOL.append(p1_pool)


        top[0] = att_base
        rows_ring = [region(4096), region(4096), hT_flat[:, 0:4096]]
        pre0 = region(2 * 512).rearrange("p (h n) -> p h n", h=2)
        pre = region(2 * 512).rearrange("p (h n) -> p h n", h=2)
        hidden = region(2 * 1024).rearrange("p (u h n) -> p u h n", u=2, h=2)
        turned = region(2 * 1024).rearrange("p (v g j n) -> p v g j n", v=2, g=2, j=2)
        prompt_rows = region(2 * 1024).rearrange("p (v g k c) -> p v g k c", v=2, g=GROUPS, k=KT)
        cbias = region(4)
        UNITS = [(kv, b) for b in range(NB) for kv in range(2)] + [(0, None), (1, None)]
        NU = len(UNITS)
        rows_in = [sem(f"cmp_rows{i}_in") for i in range(3)]
        prompt_in = sem("cmp_prompt_rows_in")
        turned_done = sem("cmp_turned")
        c_bias_mm, c_bias = sem("cmp_bias_product"), sem("cmp_bias")
        c_mm, c_first, c_pre, c_hid = [sem(f"cmp_{n}") for n in ("products", "first_taken", "summed", "hidden")]
        c_out, c_out_k, c_out_v = [sem(f"cmp_{n}") for n in ("out", "k_taken", "v_taken")]
        kn_sq, kn_ss, kn_rt, kn_r, kn_bc = [sem(f"kc_{n}") for n in
                                                    ("squared", "summed", "root", "rstd", "spread")]

        def unit_columns(u):
            return (CHUNKS, NC) if UNITS[u][1] is not None else (PCH, NCP)

        def p2_sp(sp):
            load_slots(sp, "w1", t["w1"], 4)
            sp.wait_ge(pages_in, 16)
            for u in range(2 * NB):
                kv, b = UNITS[u]
                if u == 0:
                    sp.wait_ge(n_ss, 1)
                if u == 2:
                    sp.wait_ge(met, 4)
                if u >= 3:
                    sp.wait_ge(c_mm, 2 * (u - 2))
                with sp.Fori(0, NPAGE) as i:
                    page = sp.value_load(pages[0:1, bass.ds(i + b * NPAGE, 1)], min_val=0, max_val=NPHYS - 1)
                    sp.dma_start(rows_ring[u % 3].rearrange("p (i n) -> p i n", i=NPAGE)[:, bass.ds(i, 1)],
                                 t["cmp_pages"][bass.ds(page, 1), kv].rearrange("o p n -> p o n")
                                 ).then_inc(rows_in[u % 3], 16)
        SP.append(p2_sp)

        def p2_pe(pe):
            for i in range(4):
                slot_wait(pe, slot_at["w1"] + i)
            base = slot_at["w1"]
            pe_cols = par[:, PAR["pe"]].rearrange("p (v m k) -> p v m k", v=2, m=2)

            def w1(kv, m, kt, ht):
                s = (base + 2 * kv + m) % RING
                return ring[:, s, kt * 256 + ht * P:kt * 256 + (ht + 1) * P]

            for kv in range(2):
                for ht in range(2):
                    for m in range(2):
                        for kt in range(KT):
                            last = pe.matmul(ps[:, 7, 2 * kv + ht:2 * kv + ht + 1], w1(kv, m, kt, ht),
                                             pe_cols[:, kv, m, kt:kt + 1], start=m + kt == 0,
                                             stop=m == 1 and kt == KT - 1)
            last.then_inc(c_bias_mm, 1)

            w2 = par[:, PAR["w2"]].rearrange("p (v h n) -> p v h n", v=2, h=2)

            def second(u):
                kv, b = UNITS[u]
                n = unit_columns(u)[1]
                pe.wait_ge(c_hid, 2 * (u + 1))
                if u == 1:
                    pe.wait_ge(c_bias, 1)
                if u >= 2:
                    pe.wait_ge(c_out_v if kv else c_out_k, u // 2)
                hid = hidden[:, u % 2, :, 0:GROUPS * n].rearrange("p h (g n) -> p h g n", g=GROUPS)
                for g in range(GROUPS):
                    for ht in range(2):
                        if kv == 0:
                            a = g % 2
                            last = pe.matmul(ps[a * HD:(a + 1) * HD, 6, (g // 2) * n:(g // 2 + 1) * n],
                                             w2[:, 0, ht], hid[:, ht, g], start=ht == 0, stop=ht == 1)
                        else:
                            last = pe.matmul(ps[0:n, 7, g * HD:(g + 1) * HD], hid[:, ht, g], w2[:, 1, ht],
                                             start=ht == 0, stop=ht == 1)
                last.then_inc(c_out, 1)

            for u, (kv, b) in enumerate(UNITS):
                n = unit_columns(u)[0]
                if b is None:
                    if kv == 0:
                        pe.wait_ge(prompt_in, 16 * 16)
                    cols = prompt_rows[:, kv].rearrange("p g k c -> p k g c")
                else:
                    pe.wait_ge(rows_in[u % 3], 16 * NPAGE * (u // 3 + 1))
                    cols = rows_ring[u % 3].rearrange("p (i g k c) -> p k g i c", i=NPAGE, g=GROUPS, k=KT)
                for ht in range(2):
                    q = (2 * u + ht) % 3
                    k = 2 * u + ht - 3
                    if k >= 0:
                        pe.wait_ge(c_first, k + 1)
                        pe.wait_ge(c_pre, k + 1)
                    for m in range(2):
                        for kt in range(KT):
                            last = pe.matmul(ps[:, 2 * q + m, 0:GROUPS * n], w1(kv, m, kt, ht), cols[:, kt],
                                             start=kt == 0, stop=kt == KT - 1)
                    last.then_inc(c_mm, 1)
                if u >= 1:
                    second(u - 1)
            pe.wait_ge(c_mm, 2 * NU)
            for i in range(4):
                pe.sem_inc(w_used, 1)
            second(NU - 1)

            for b in range(NB):
                for gp in range(2):
                    j = 2 * b + gp
                    pe.wait_ge(kn_sq, 1)
                    last = pe.matmul(ps[0:32, 0, 0:NC], window[:, 34 - 2 * j:66 - 2 * j], kc_sq[:, b, gp],
                                     start=j == 0, stop=j == 15)
            for gp in range(2):
                last = pe.matmul(ps[0:4, 1, 0:NCP], window[:, 34 - 2 * gp:38 - 2 * gp], kc_sq_p[:, gp],
                                 start=gp == 0, stop=gp == 1)
            last.then_inc(kn_ss, 1)
            pe.wait_ge(kn_r, 2)
            for b in range(NB):
                for gp in range(2):
                    for a in range(2):
                        r = 2 * (2 * b + gp) + a
                        last = pe.matmul(ps[a * HD:(a + 1) * HD, 2 + b // 2, (b % 2 * 2 + gp) * P:(b % 2 * 2 + gp) * P + NC],
                                         ident[0:32, r:r + 1].to_broadcast([32, HD]), kn_rows[0:32, 0, 0:NC],
                                         start=True, stop=True)
                if b % 2:
                    last.then_inc(kn_bc, 1)
            for gp in range(2):
                for a in range(2):
                    last = pe.matmul(ps[a * HD:(a + 1) * HD, 6, gp * NCP:(gp + 1) * NCP],
                                     ident[0:4, 2 * gp + a:2 * gp + a + 1].to_broadcast([4, HD]),
                                     kn_rows[0:4, 1, 0:NCP], start=True, stop=True)
            last.then_inc(kn_bc, 1)
            meet(pe, 2)
        PE.append(p2_pe)

        kc_sq = rows_ring[0][:, 0:NB * 2 * NC].rearrange("p (b g n) -> p b g n", b=NB, g=2)
        kc_sq_p = rows_ring[0][:, 3000:3000 + 2 * NCP].rearrange("p (g n) -> p g n", g=2)
        kn_rows = rows_ring[0][:, 3500:3500 + 256].rearrange("p (x n) -> p x n", x=2)

        def p2_act(act):
            do = act_do
            act.wait_ge(c_bias_mm, 1)
            do(act.activation(cbias, ps[:, 7, 0:4], ACT.Copy), c_bias)
            for u, (kv, b) in enumerate(UNITS):
                n, nb = unit_columns(u)
                for ht in range(2):
                    k = 2 * u + ht
                    act.wait_ge(c_mm, k + 1)
                    if k >= 2:
                        act.wait_ge(c_pre, k - 1)
                    do(act.activation(pre0[:, ht, 0:GROUPS * n], ps[:, 2 * (k % 3), 0:GROUPS * n], ACT.Identity,
                                      bias=cbias[:, 2 * kv + ht:2 * kv + ht + 1]), c_first)
                for ht in range(2):
                    k = 2 * u + ht
                    act.wait_ge(c_pre, k + 1)
                    if u >= 2 and ht == 0:
                        act.wait_ge(c_out, u - 1)
                    do(act.activation(hidden[:, u % 2, ht, 0:GROUPS * nb], pre[:, ht, 0:GROUPS * nb], ACT.Silu), c_hid)
                if kv == 1 and u >= 2:
                    take_v(act, do, u - 2)
            take_v(act, do, NU - 1)
            act.wait_ge(c_out_k, NB + 1)
            act.wait_ge(c_mm, 2 * NU)
            do(act.activation(kc_sq, kcT, ACT.Square))
            do(act.activation(kc_sq_p, kcP, ACT.Square), kn_sq)
            act.wait_ge(kn_ss, 1)
            do(act.activation(kn_rows[0:32, 0, 0:NC], ps[0:32, 0, 0:NC], ACT.Sqrt, bias=eps[0:32], scale=1.0 / HD), kn_rt)
            do(act.activation(kn_rows[0:4, 1, 0:NCP], ps[0:4, 1, 0:NCP], ACT.Sqrt, bias=eps[0:4], scale=1.0 / HD), kn_rt)
            meet(act, 2)
        ACTE.append(p2_act)

        def take_v(act, do, u):
            b = UNITS[u][1]
            act.wait_ge(c_out, u + 1)
            if b is None:
                do(act.activation(vcP[0:NCP], ps[0:NCP, 7, 0:256], ACT.Copy), c_out_v)
            else:
                do(act.activation(vcS[0:NC, b], ps[0:NC, 7, 0:256], ACT.Copy), c_out_v)

        def p2_dve(dve):
            do = dve_do
            for kv, name in enumerate(("kc", "vc")):
                for gp in range(2):
                    src = kvT[:, KV_TILE[name] + gp, 0:SEQ].rearrange("p (c k j) -> p j k c", k=KT, j=2)
                    for j in range(2):
                        do(dve.tensor_copy(turned[:, kv, gp, j].rearrange("p (k c) -> p k c", k=KT), src[:, j]),
                           turned_done)
            for u, (kv, b) in enumerate(UNITS):
                n, nb = unit_columns(u)
                for ht in range(2):
                    k = 2 * u + ht
                    dve.wait_ge(c_first, k + 1)
                    if k >= 2:
                        dve.wait_ge(c_hid, k - 1)
                    if k == 0:
                        dve.wait_ge(c_mm, 1)
                    shape = dict(g=GROUPS)
                    do(dve.tensor_tensor(pre[:, ht, 0:GROUPS * nb].rearrange("p (g n) -> p g n", **shape),
                                         pre0[:, ht, 0:GROUPS * n].rearrange("p (g n) -> p g n", **shape)[:, :, 0:nb],
                                         ps[:, 2 * (k % 3) + 1, 0:GROUPS * n].rearrange("p (g n) -> p g n", **shape)[:, :, 1:n],
                                         ALU.add), c_pre)
                if kv == 1:
                    take_k(dve, do, u - 1)
            dve.wait_ge(kn_rt, 2)
            do(dve.reciprocal(kn_rows[0:32, 0, 0:NC], kn_rows[0:32, 0, 0:NC]), kn_r)
            do(dve.reciprocal(kn_rows[0:4, 1, 0:NCP], kn_rows[0:4, 1, 0:NCP]), kn_r)
            g = par[:, PAR["qk"]][:, 1:2]
            for i in range(NB // 2):
                dve.wait_ge(kn_bc, i + 1)
                k2 = kcT[:, 2 * i:2 * i + 2].rearrange("p b g n -> p (b g) n")
                do(dve.scalar_tensor_tensor(k2, k2, g, ps[:, 2 + i].rearrange("p (x n) -> p x n", x=4)[:, :, 0:NC],
                                            ALU.mult, ALU.mult))
            dve.wait_ge(kn_bc, NB // 2 + 1)
            kp = kcP.rearrange("p g n -> p (g n)")
            do(dve.scalar_tensor_tensor(kp, kp, g, ps[:, 6, 0:2 * NCP], ALU.mult, ALU.mult))
            meet(dve, 2)
        DVE.append(p2_dve)

        def take_k(dve, do, u):
            b = UNITS[u][1]
            nb = unit_columns(u)[1]
            dve.wait_ge(c_out, u + 1)
            dst = kcP if b is None else kcT[:, b]
            do(dve.tensor_copy(dst, ps[:, 6, 0:2 * nb].rearrange("p (g n) -> p g n", g=2)), c_out_k)

        def p2_pool(pool):
            pool.wait_ge(turned_done, 8)
            for kv in range(2):
                for g in range(GROUPS):
                    a = g % 2
                    for j in range(2):
                        pool.dma_start(prompt_rows[j * HD:(j + 1) * HD, kv, g],
                                       turned[a * HD:(a + 1) * HD, kv, g // 2, j].rearrange("p (k c) -> p k c", k=KT)
                                       ).then_inc(prompt_in, 16)
            meet(pool, 2)
        POOL.append(p2_pool)

        top[0] = att_base
        cn = region(CONST_N["own_head"].start)
        cn_ = lambda name: cn[:, CONST_N[name]]
        after_cn = top[0]
        vtok = region(2 * QT * 256).rearrange("p (b i n) -> p b i n", b=2, i=QT)
        S_ring = region(4 * SEQ).rearrange("p (x n) -> p x n", x=4)
        PT_ring = region(4 * SEQ).rearrange("p (x n) -> p x n", x=4)
        low = region(4 * 4).rearrange("p (w x) -> p w x", w=4)
        Sc = region(HEADS * NCP)
        cmp_small = region(4 * HEADS).rearrange("p (w h) -> p w h", w=4)
        PTc = region(2 * HEADS * P).rearrange("p (x h n) -> p x h n", x=2, h=HEADS)
        ITEMS = [(i, gp, r, a, br) for i in range(QT) for gp in range(2) for r in range(4) for a in range(2)
                 for br in range(2)]
        PER_TILE = len(ITEMS) // QT
        BR_K, BR_V = ("ks", "kw"), ("vs", "vw")
        a_vt, a_vev = sem("v_turned"), sem("v_taken")
        a_mm, a_s, a_exp, a_p, a_t, a_pt, a_pv = [sem(f"prompt_{n}") for n in (
            "scores", "biased", "exp", "weights", "turned", "turned_taken", "values")]
        a_o = sem("prompt_out_taken")
        pc_mm, pc_s, pc_e, pc_p, pc_t, pc_pt = [sem(f"prompt_cmp_{n}") for n in (
            "scores", "biased", "exp", "weights", "turned", "turned_taken")]

        def cols_of(i):
            return (i + 1) * P

        def p3_sp(sp):
            sp.wait_ge(met, 8)
            sp.dma_start(cn, t["const_n"][:, 0:CONST_N["own_head"].start]).then_inc(cn_in, 16)
        SP.append(p3_sp)

        def p3_pe(pe):
            for br in range(2):
                for gp in range(2):
                    k = 2 * br + gp
                    for i in range(QT):
                        last = pe.transpose(ps[:, k, i * P:(i + 1) * P],
                                            kvT[:, KV_TILE[BR_V[br]] + gp, i * P:(i + 1) * P], ident)
                    last.then_inc(a_vt, 1)
            for br in range(2):
                for gp in range(2):
                    last = pe.transpose(ps[0:NS, 4, (2 * br + gp) * P:(2 * br + gp + 1) * P],
                                        kvT[:, KV_TILE[BR_V[br]] + gp, SEQ:NT], ident)
            last.then_inc(a_vt, 1)
            pe.wait_ge(a_vev, 5)

            def cmp_scores(i):
                if i >= 1:
                    pe.wait_ge(pc_pt, 4 * i)
                for a in range(2):
                    if a == 1:
                        pe.wait_ge(pc_mm, 2 * i + 1)
                    for kt in range(KT):
                        hh = 2 * kt + a
                        h0 = a * HD
                        last = pe.matmul(ps[:, 7, hh * NCP:(hh + 1) * NCP], qT[h0:h0 + HD, kt, i * P:(i + 1) * P],
                                         kcP[h0:h0 + HD, kt // 4], start=True, stop=True)
                    last.then_inc(pc_mm, 1)

            def cmp_turn(i, k):
                pe.wait_ge(pc_p, i + 1)
                if k >= 1:
                    pe.wait_ge(pc_pt, 4 * i + k)
                for j in range(4):
                    hh = 4 * k + j
                    last = pe.transpose(ps[0:NCP, 7, j * P:(j + 1) * P], Sc[:, hh * NCP:(hh + 1) * NCP], ident)
                last.then_inc(pc_t, 1)

            def scores(n):
                i, gp, r, a, br = ITEMS[n]
                if n >= 3:
                    pe.wait_ge(a_s, n - 2)
                h0 = a * HD
                pe.matmul(ps[:, n % 3, 0:cols_of(i)], qT[h0:h0 + HD, gp * 4 + r, i * P:(i + 1) * P],
                          kvT[h0:h0 + HD, KV_TILE[BR_K[br]] + gp, 0:cols_of(i)], start=True, stop=True
                          ).then_inc(a_mm, 1)

            def turn(n):
                i = ITEMS[n][0]
                pe.wait_ge(a_p, n + 1)
                if n >= 2:
                    pe.wait_ge(a_pt, n - 1)
                for j in range(i + 1):
                    last = pe.transpose(ps[:, 3 + n % 2, j * P:(j + 1) * P], S_ring[:, n % 4, j * P:(j + 1) * P], ident)
                last.then_inc(a_t, 1)

            def values(n):
                i, gp, r, a, br = ITEMS[n]
                grp = 2 * i + gp
                out = ps[a * HD:(a + 1) * HD, 5 + grp % 2, r * P:(r + 1) * P]
                c0 = (2 * gp + a) * HD
                if br == 0:
                    if r + a == 0 and grp >= 2:
                        pe.wait_ge(a_o, grp - 1)
                    hh = 2 * (gp * 4 + r) + a
                    pe.wait_ge(pc_pt, 4 * i + hh // 4 + 1)
                    pe.matmul(out, vcP[0:NCP, c0:c0 + HD], PTc[0:NCP, i % 2, hh], start=True, stop=False)
                pe.wait_ge(a_pt, n + 1)
                for j in range(i + 1):
                    last = pe.matmul(out, vtok[:, br, j, c0:c0 + HD], PT_ring[:, n % 4, j * P:(j + 1) * P],
                                     start=False, stop=br == 1 and j == i)
                last.then_inc(a_pv, 1)

            cmp_scores(0)
            for k in range(4):
                cmp_turn(0, k)
            for n in range(len(ITEMS) + 3):
                i, k = n // PER_TILE + 1, n % PER_TILE
                if i < QT and k == 6:
                    cmp_scores(i)
                if i < QT and 14 <= k < 30 and k % 4 == 2:
                    cmp_turn(i, (k - 14) // 4)
                if n < len(ITEMS):
                    scores(n)
                if 2 <= n < len(ITEMS) + 2:
                    turn(n - 2)
                if n >= 3:
                    values(n - 3)
            meet(pe, 3)
        PE.append(p3_pe)

        def p3_act(act):
            do = act_do
            for k in range(4):
                act.wait_ge(a_vt, k + 1)
                br, gp = k // 2, k % 2
                do(act.activation(vtok[:, br, :, gp * P:(gp + 1) * P], ps[:, k].rearrange("p (i n) -> p i n", i=QT),
                                  ACT.Copy), a_vev)
            act.wait_ge(a_vt, 5)
            do(act.activation(vnew[0:NS], ps[0:NS, 4].rearrange("p (b n) -> p b n", b=2), ACT.Copy), a_vev)

            def cmp_exp(i):
                act.wait_ge(pc_s, i + 1)
                do(act.activation(Sc, Sc, ACT.Exp), pc_e)

            def cmp_take(i, k):
                act.wait_ge(pc_t, 4 * i + k + 1)
                do(act.activation(PTc[0:NCP, i % 2, 4 * k:4 * k + 4], ps[0:NCP, 7].rearrange("p (h n) -> p h n", h=4),
                                  ACT.Copy), pc_pt)

            cmp_exp(0)
            for k in range(4):
                cmp_take(0, k)
            for n in range(len(ITEMS) + 3):
                i, k = n // PER_TILE + 1, n % PER_TILE
                if i < QT and k == 9:
                    cmp_exp(i)
                if i < QT and 14 <= k < 30 and k % 4 == 2:
                    cmp_take(i, (k - 14) // 4)
                if n < len(ITEMS):
                    w = cols_of(ITEMS[n][0])
                    act.wait_ge(a_s, n + 1)
                    do(act.activation(S_ring[:, n % 4, 0:w], S_ring[:, n % 4, 0:w], ACT.Exp, bias=low[:, 0, n % 4:n % 4 + 1],
                                      scale=-1.0, accum_out=low[:, 1, n % 4:n % 4 + 1]), a_exp)
                if 2 <= n < len(ITEMS) + 2:
                    m = n - 2
                    w = cols_of(ITEMS[m][0])
                    act.wait_ge(a_t, m + 1)
                    if m >= 4:
                        act.wait_ge(a_pv, m - 3)
                    do(act.activation(PT_ring[:, m % 4, 0:w], ps[:, 3 + m % 2, 0:w], ACT.Copy), a_pt)
                if n >= 3 and (n - 3) % 16 == 15:
                    grp = (n - 3) // 16
                    i, gp = grp // 2, grp % 2
                    act.wait_ge(a_pv, n - 2)
                    do(act.activation(qT[:, gp * 4:gp * 4 + 4, i * P:(i + 1) * P],
                                      ps[:, 5 + grp % 2].rearrange("p (r n) -> p r n", r=4), ACT.Copy), a_o)
            meet(act, 3)
        ACTE.append(p3_act)

        def p3_dve(dve):
            do = dve_do
            dve.wait_ge(cn_in, 32)
            hs = dict(h=HEADS)
            Sc3 = Sc.rearrange("p (h n) -> p h n", **hs)

            def cmp_bias(i):
                dve.wait_ge(pc_mm, 2 * i + 2)
                if i >= 1:
                    dve.wait_ge(pc_t, 4 * i)
                dist = cn_("dist_c")[:, i * NCP:(i + 1) * NCP].unsqueeze(1).to_broadcast([P, HEADS, NCP])
                do(dve.tensor_tensor(Sc3, ps[:, 7, 0:HEADS * NCP].rearrange("p (h n) -> p h n", **hs), dist, ALU.add))
                do(dve.tensor_tensor(Sc, Sc, cn_("slope_c"), ALU.mult))
                do(dve.tensor_reduce(cmp_small[:, 0], Sc3, AX.X, ALU.max))
                do(dve.tensor_tensor(Sc3, Sc3, cmp_small[:, 0].unsqueeze(2).to_broadcast([P, HEADS, NCP]),
                                     ALU.subtract), pc_s)

            def cmp_weights(i):
                dve.wait_ge(pc_e, i + 1)
                do(dve.tensor_reduce(cmp_small[:, 1], Sc3, AX.X, ALU.add))
                do(dve.reciprocal(cmp_small[:, 2], cmp_small[:, 1]))
                g = gates[:, i, 0:HEADS].rearrange("p (g a r) -> p g r a", g=2, a=2)
                for gp in range(2):
                    do(dve.tensor_tensor(cmp_small[:, 3, gp * 8:(gp + 1) * 8].rearrange("p (r a) -> p r a", r=4),
                                         cmp_small[:, 2, gp * 8:(gp + 1) * 8].rearrange("p (r a) -> p r a", r=4),
                                         g[:, gp], ALU.mult))
                do(dve.tensor_tensor(Sc3, Sc3, cmp_small[:, 3].unsqueeze(2).to_broadcast([P, HEADS, NCP]), ALU.mult))
                seen = cn_("seen_c")[:, i * NCP:(i + 1) * NCP].unsqueeze(1).to_broadcast([P, HEADS, NCP])
                do(dve.tensor_tensor(Sc3, Sc3, seen, ALU.mult), pc_p)

            cmp_bias(0)
            cmp_weights(0)
            slope = slopes()
            for n in range(len(ITEMS) + 1):
                i, k = n // PER_TILE + 1, n % PER_TILE
                if i < QT and k == 8:
                    cmp_bias(i)
                if i < QT and k == 11:
                    cmp_weights(i)
                if n < len(ITEMS):
                    i, gp, r, a, br = ITEMS[n]
                    w = cols_of(i)
                    dve.wait_ge(a_mm, n + 1)
                    if n >= 4:
                        dve.wait_ge(a_t, n - 3)
                    do(dve.tensor_tensor_reduce(S_ring[:, n % 4, 0:w], ps[:, n % 3, 0:w], cn_("dist")[:, SEQ - w:SEQ],
                                                -float(slope[head_of(gp * 4 + r, a)]), 3e38, ALU.add, ALU.min,
                                                low[:, 0, n % 4:n % 4 + 1]), a_s)
                if n >= 1:
                    m = n - 1
                    i, gp, r, a, br = ITEMS[m]
                    h = (2 * gp + a) * 4 + r
                    S_ = S_ring[:, m % 4, 0:cols_of(i)]
                    dve.wait_ge(a_exp, m + 1)
                    do(dve.reciprocal(low[:, 2, m % 4:m % 4 + 1], low[:, 1, m % 4:m % 4 + 1]))
                    c = (1 + br) * HEADS + h
                    do(dve.tensor_scalar(S_, S_, low[:, 2, m % 4:m % 4 + 1], gates[:, i, c:c + 1], ALU.mult, ALU.mult), a_p)
            meet(dve, 3)
        DVE.append(p3_dve)

        def p3_pool(pool):
            pool.wait_ge(pages_in, 16)
            pool.wait_ge(w_used, slot_at["w1"] + 4)
            p4_load_unit(pool, 1, 1)
            pool.wait_ge(a_vev, 5)
            pool.wait_ge(stored, 16)
            p4_load_unit(pool, 3, 1)
            meet(pool, 3)
        POOL.append(p3_pool)

        top[0] = after_cn
        q_diag = region(2 * NB * 32).rearrange("p (g b n) -> p g b n", g=2, b=NB)
        win = region(2 * 2048).rearrange("p (b n) -> p b n", b=2)
        ali = region(PAST)
        S = region(PAST + NS)
        PT = region((NPAGE + 1) * P).rearrange("p (j n) -> p j n", j=NPAGE + 1)
        Sw = region(SEQ + NS)
        PTw = region(5 * P).rearrange("p (j n) -> p j n", j=5)
        PTcs = region(PAIRS * P).rearrange("p (i n) -> p i n", i=PAIRS)
        sel_bias = region(PAIRS * NBLK).rearrange("p (i s) -> p i s", i=PAIRS)
        few = region(12 * PAIRS).rearrange("p (w i) -> p w i", w=12)
        late = top[0]
        Sc4 = S[:, 0:PAIRS * NC].rearrange("p (i n) -> p i n", i=PAIRS)
        weights_c = S[:, 512:512 + PAIRS * NC].rearrange("p (i n) -> p i n", i=PAIRS)
        imp = S[:, 1024:1024 + PAIRS * (NC + 2)].rearrange("p (i n) -> p i n", i=PAIRS)
        chunk_p = PT.rearrange("p j n -> p (j n)")[:, 0:PAIRS * CHUNKS].rearrange("p (i n) -> p i n", i=PAIRS)
        block_p = S[:, 1600:1600 + PAIRS * NBLK].rearrange("p (i s) -> p i s", i=PAIRS)
        rank = S[:, 1760:1760 + FREE_BLOCKS]
        above = PT.rearrange("p j n -> p (j n)")[:, 512:512 + FREE_BLOCKS ** 2].rearrange("p (s o) -> p s o", s=FREE_BLOCKS)
        equal = win[:, 1, 0:FREE_BLOCKS ** 2].rearrange("p (s o) -> p s o", s=FREE_BLOCKS)
        dead_kv = kvT_flat[:, 0:8 * NT]
        UNIT = [ring[:, 0:2].rearrange("p s n -> p (s n)"), ring[:, 2:4].rearrange("p s n -> p (s n)"),
                hT_flat[:, 0:4096], dead_kv[:, 0:4096]]
        K_of = [UNIT[b].rearrange("p (i g n) -> p i g n", i=NPAGE, g=2) for b in range(2)]
        V_of = [UNIT[2 + b].rearrange("p (i n) -> p i n", i=NPAGE) for b in range(2)]
        win_k = [win[:, b, 0:1024].rearrange("p (g n) -> p g n", g=2) for b in range(2)]
        win_v = [win[:, b, 1024:2048].rearrange("p (j n) -> p j n", j=QT) for b in range(2)]
        unit_in = [sem(f"sel_{n}_in") for n in ("k0", "k1", "v0", "v1")]
        win_in = [sem("win0_in"), sem("win1_in")]
        win_stored = sem("win_stored")
        s_diag = sem("q_diag_done")
        sc_mm, sc_s, sc_e, sc_w, sc_imp, sc_t, sc_pt, sc_sel = [sem(f"sample_cmp_{n}") for n in (
            "scores", "biased", "exp", "weights", "importance", "turned", "turned_taken", "selected")]
        ss_mm, ss_s1, ss_s, ss_e, ss_p, ss_t, ss_pt, ss_pv, ss_o = [sem(f"sample_sel_{n}") for n in (
            "scores", "scores_taken", "biased", "exp", "weights", "turned", "turned_taken", "values", "out_taken")]
        sw_mm, sw_s1, sw_s, sw_e, sw_p, sw_t, sw_pt = [sem(f"sample_win_{n}") for n in (
            "scores", "scores_taken", "biased", "exp", "weights", "turned", "turned_taken")]
        TURNS = [(0, 4), (4, 8), (8, 12), (12, 16), (16, 17)]

        def p4_load_unit(sp, x, b):
            src = t["sel_k"] if x < 2 else t["sel_v"]
            dst = UNIT[x].rearrange("p (i n) -> p i n", i=NPAGE)
            with sp.Fori(0, NPAGE) as i:
                page = sp.value_load(pages[0:1, bass.ds(i + b * NPAGE, 1)], min_val=0, max_val=NPHYS - 1)
                sp.dma_start(dst[:, bass.ds(i, 1)], src[bass.ds(page, 1)].rearrange("o p n -> p o n")
                             ).then_inc(unit_in[x], 16)

        def p4_sp(sp):
            sp.wait_ge(w_used, slot_at["w1"] + 4)
            for pr in range(PAIRS):
                for x in (0, 2):
                    if pr >= 1:
                        sp.wait_ge(ss_mm if x < 2 else ss_pv, pr)
                    p4_load_unit(sp, x, 2 * pr)
                if pr == 0:
                    sp.wait_ge(met, 12)
                    sp.dma_start(ali, t["const_ali"]).then_inc(ali_in, 16)
                for b in range(2):
                    if pr >= 1 and b == 0:
                        sp.wait_ge(ss_pv, pr)
                        sp.wait_ge(win_stored, 32 * pr)
                    if pr == 0 and b == 1:
                        sp.wait_ge(sc_sel, 1)
                    sp.dma_start(win[:, b], t["win"][2 * pr + b]).then_inc(win_in[b], 16)
        SP.append(p4_sp)

        def rows32(bb, gp):
            return slice(bb * HD + gp * 32, bb * HD + (gp + 1) * 32)

        def p4_pe(pe):
            pe.wait_ge(s_diag, 4)
            for pr in range(PAIRS):
                for bb in range(2):
                    for gp in range(2):
                        b = 2 * pr + bb
                        last = pe.matmul(ps[rows32(bb, gp), 5, pr * NC:(pr + 1) * NC], q_diag[:, gp, b], kcT[:, b, gp],
                                         start=True, stop=True)
            last.then_inc(sc_mm, 1)

            def scores(pr):
                for x in range(2):
                    pe.wait_ge(unit_in[x], 16 * NPAGE * (pr + 1))
                if pr >= 1:
                    pe.wait_ge(ss_s1, pr)
                    pe.wait_ge(sw_s1, pr)
                for bb in range(2):
                    for gp in range(2):
                        q, r = q_diag[:, gp, 2 * pr + bb], rows32(bb, gp)
                        for j in range(4):
                            last = pe.matmul(ps[r, j, :], q, K_of[bb][:, 4 * j:4 * j + 4, gp], start=True, stop=True)
                last.then_inc(ss_mm, 1)
                for bb in range(2):
                    for gp in range(2):
                        q, r = q_diag[:, gp, 2 * pr + bb], rows32(bb, gp)
                        pe.matmul(ps[r, 4, 0:NS], q, kvT[:, KV_TILE["ks"] + gp, SEQ:NT], start=True, stop=True)
                        last = pe.matmul(ps[r, 4, NS:2 * NS], q, kvT[:, KV_TILE["kw"] + gp, SEQ:NT],
                                         start=True, stop=True)
                last.then_inc(sw_mm, 1)

            def win_scores(pr):
                if pr == 0:
                    pe.wait_ge(sc_s, 1)
                else:
                    pe.wait_ge(ss_o, 4 * pr)
                for bb in range(2):
                    pe.wait_ge(win_in[bb], 16 * (pr + 1))
                    for gp in range(2):
                        last = pe.matmul(ps[rows32(bb, gp), 5, :], q_diag[:, gp, 2 * pr + bb], win_k[bb][:, gp],
                                         start=True, stop=True)
                last.then_inc(sw_mm, 1)

            pe.wait_ge(sc_w, 1)
            pe.matmul(ps[:, 6, 0:PAIRS * NC], cn_("same_gt"), weights_c.rearrange("p i n -> p (i n)"), start=True,
                      stop=True).then_inc(sc_imp, 1)
            pe.wait_ge(sc_w, 2)
            for pr in range(PAIRS):
                last = pe.transpose(ps[0:NC, 7, pr * P:(pr + 1) * P], Sc4[:, pr], ident)
            last.then_inc(sc_t, 1)
            scores(0)
            for pr in range(PAIRS):
                win_scores(pr)
                pe.wait_ge(sw_p, pr + 1)
                if pr == 0:
                    pe.wait_ge(sc_pt, 1)
                    pe.wait_ge(sc_sel, 1)
                else:
                    pe.wait_ge(ss_pt, 5 * pr)
                for j in range(4):
                    last = pe.transpose(ps[:, 6, j * P:(j + 1) * P], Sw[:, j * P:(j + 1) * P], ident)
                last.then_inc(sw_t, 1)
                pe.transpose(ps[0:NS, 7, 0:P], Sw[:, SEQ:SEQ + NS], ident).then_inc(sw_t, 1)
                pe.wait_ge(ss_p, pr + 1)
                for k, (j0, j1) in enumerate(TURNS):
                    if k >= 2:
                        pe.wait_ge(ss_pt, 5 * pr + k - 1)
                    else:
                        pe.wait_ge(sw_pt, 2 * pr + k + 1)
                    n = P if k < 4 else NS
                    for j in range(j0, j1):
                        last = pe.transpose(ps[0:n, 6 + k % 2, (j - j0) * P:(j - j0 + 1) * P], S[:, j * P:j * P + n], ident)
                    last.then_inc(ss_t, 1)
                if pr + 1 < PAIRS:
                    scores(pr + 1)
                pe.wait_ge(ss_pt, 5 * pr + 5)
                for x in range(2):
                    pe.wait_ge(unit_in[2 + x], 16 * NPAGE * (pr + 1))
                for bb in range(2):
                    b = 2 * pr + bb
                    for gp in range(2):
                        r, c = rows32(bb, gp), slice(gp * P, (gp + 1) * P)
                        out = ps[:, 5, r]
                        pe.matmul(out, vcS[0:NC, b, c], PTcs[0:NC, pr, r], start=True, stop=False)
                        for j in range(4):
                            pe.matmul(out, win_v[bb][:, j, c], PTw[:, j, r], start=False, stop=False)
                        pe.matmul(out, vnew[0:NS, 1, c], PTw[0:NS, 4, r], start=False, stop=False)
                        for j in range(NPAGE):
                            pe.matmul(out, V_of[bb][:, j, c], PT[:, j, r], start=False, stop=False)
                        last = pe.matmul(out, vnew[0:NS, 0, c], PT[0:NS, NPAGE, r], start=False, stop=True)
                last.then_inc(ss_pv, 1)
            meet(pe, 4)
        PE.append(p4_pe)

        def p4_act(act):
            do = act_do
            act.wait_ge(sc_s, 1)
            do(act.activation(Sc4, Sc4, ACT.Exp), sc_e)
            act.wait_ge(sc_t, 1)
            do(act.activation(PTcs[0:NC], ps[0:NC, 7].rearrange("p (i n) -> p i n", i=PAIRS), ACT.Copy), sc_pt)
            for pr in range(PAIRS):
                act.wait_ge(sw_s, pr + 1)
                do(act.activation(Sw, Sw, ACT.Exp, bias=few[:, 4, pr:pr + 1], accum_out=few[:, 5, pr:pr + 1]), sw_e)
                act.wait_ge(ss_s, pr + 1)
                do(act.activation(S, S, ACT.Exp, bias=few[:, 8, pr:pr + 1], accum_out=few[:, 9, pr:pr + 1]), ss_e)
                if pr >= 1:
                    act.wait_ge(ss_pv, pr)
                act.wait_ge(sw_t, 2 * pr + 1)
                do(act.activation(PTw[:, 0:4], ps[:, 6].rearrange("p (j n) -> p j n", j=4), ACT.Copy), sw_pt)
                act.wait_ge(sw_t, 2 * pr + 2)
                do(act.activation(PTw[0:NS, 4], ps[0:NS, 7, 0:P], ACT.Copy), sw_pt)
                for k, (j0, j1) in enumerate(TURNS):
                    act.wait_ge(ss_t, 5 * pr + k + 1)
                    n = P if k < 4 else NS
                    do(act.activation(PT[0:n, j0:j1], ps[0:n, 6 + k % 2, 0:(j1 - j0) * P].rearrange(
                        "p (j n) -> p j n", j=j1 - j0), ACT.Copy), ss_pt)
                act.wait_ge(ss_pv, pr + 1)
                for a in range(2):
                    for bb in range(2):
                        h0 = a * HD
                        src = ps[h0:h0 + HD, 5, bb * HD:(bb + 1) * HD].rearrange(
                            "p (g a r t) -> p a g r t", g=2, a=2, r=4)[:, a]
                        c0 = SEQ + (2 * pr + bb) * TS
                        do(act.activation(qT[h0:h0 + HD, :, c0:c0 + TS].rearrange("p (g r) t -> p g r t", g=2), src,
                                          ACT.Copy), ss_o)
            meet(act, 4)
        ACTE.append(p4_act)

        def p4_dve(dve):
            do = dve_do
            do(dve.memset(q_diag, 0.0))
            for a in range(2):
                h0 = a * HD
                for gp in range(2):
                    src = qT[h0:h0 + HD, gp * 4:gp * 4 + 4, SEQ:NT].rearrange("p r (b t) -> p b r t", b=NB)
                    do(dve.tensor_copy(q_diag[h0:h0 + HD, gp, :, a * 16:(a + 1) * 16].rearrange(
                        "p b (r t) -> p b r t", r=4), src), s_diag)
            p3 = [P, PAIRS, NC]
            dve.wait_ge(sc_mm, 1)
            do(dve.tensor_tensor(Sc4, ps[:, 5, 0:PAIRS * NC].rearrange("p (i n) -> p i n", i=PAIRS),
                                 cn_("ali_c").unsqueeze(1).to_broadcast(p3), ALU.add))
            do(dve.tensor_reduce(few[:, 0], Sc4, AX.X, ALU.max))
            do(dve.tensor_tensor(Sc4, Sc4, few[:, 0].unsqueeze(2).to_broadcast(p3), ALU.subtract), sc_s)
            dve.wait_ge(sc_e, 1)
            do(dve.tensor_reduce(few[:, 1], Sc4, AX.X, ALU.add))
            do(dve.reciprocal(few[:, 2], few[:, 1]))
            do(dve.tensor_tensor(weights_c, Sc4, few[:, 2].unsqueeze(2).to_broadcast(p3), ALU.mult), sc_w)
            do(dve.tensor_tensor(Sc4, weights_c, gate_rows[:, :, 0:1].to_broadcast(p3), ALU.mult), sc_w)
            do(dve.memset(imp, 0.0))
            dve.wait_ge(sc_imp, 1)
            do(dve.tensor_copy(imp[:, :, 1:NC + 1], ps[:, 6, 0:PAIRS * NC].rearrange("p (i n) -> p i n", i=PAIRS)))
            do(dve.tensor_tensor(chunk_p, imp[:, :, 1:NC + 2], imp[:, :, 0:NC + 1], ALU.add))
            do(dve.tensor_reduce(block_p, chunk_p.rearrange("p i (s c) -> p i s c", c=SELB // CW), AX.X, ALU.add))
            do(dve.memset(sel_bias, 0.0))
            sq = [P, FREE_BLOCKS, FREE_BLOCKS]
            for pr in range(PAIRS):
                v = block_p[:, pr, 1:NBLK - 1]
                mine, other = v.unsqueeze(2).to_broadcast(sq), v.unsqueeze(1).to_broadcast(sq)
                do(dve.tensor_tensor(above, other, mine, ALU.is_gt))
                do(dve.tensor_tensor(equal, other, mine, ALU.is_equal))
                do(dve.tensor_tensor(equal, equal, cn_("lower").rearrange("p (s o) -> p s o", s=FREE_BLOCKS), ALU.mult))
                do(dve.tensor_tensor(above, above, equal, ALU.add))
                do(dve.tensor_reduce(rank, above, AX.X, ALU.add))
                do(dve.tensor_scalar(sel_bias[:, pr, 1:NBLK - 1], rank, TAKE - 0.5, NEG, ALU.is_gt, ALU.mult),
                   sc_sel if pr == PAIRS - 1 else None)
            dve.wait_ge(ali_in, 16)
            dve.wait_ge(sc_t, 1)
            for pr in range(PAIRS):
                g = gate_rows[:, pr]
                tail = cn_("tail")[:, pr * NS:(pr + 1) * NS]
                dve.wait_ge(ss_mm, pr + 1)
                if pr >= 1:
                    dve.wait_ge(ss_t, 5 * pr)
                do(dve.tensor_tensor(S[:, 0:PAST].rearrange("p (j n) -> p j n", j=4), ps[:, 0:4],
                                     ali.rearrange("p (j n) -> p j n", j=4), ALU.add))
                dve.wait_ge(sw_mm, 2 * pr + 1)
                do(dve.tensor_tensor(S[:, PAST:PAST + NS], ps[:, 4, 0:NS], tail, ALU.add), ss_s1)
                do(dve.tensor_tensor(Sw[:, SEQ:SEQ + NS], ps[:, 4, NS:2 * NS], tail, ALU.add))
                dve.wait_ge(sw_mm, 2 * pr + 2)
                do(dve.tensor_tensor(Sw[:, 0:SEQ], ps[:, 5], cn_("ali_w"), ALU.add), sw_s1)
                do(dve.tensor_reduce(few[:, 4, pr:pr + 1], Sw, AX.X, ALU.max, negate=True), sw_s)
                S3 = S[:, 0:PAST].rearrange("p (s n) -> p s n", n=SELB)
                do(dve.tensor_tensor(S3, S3, sel_bias[:, pr].unsqueeze(2).to_broadcast([P, NBLK, SELB]), ALU.add))
                do(dve.tensor_reduce(few[:, 8, pr:pr + 1], S, AX.X, ALU.max, negate=True), ss_s)
                dve.wait_ge(sw_e, pr + 1)
                do(dve.reciprocal(few[:, 6, pr:pr + 1], few[:, 5, pr:pr + 1]))
                do(dve.tensor_scalar(Sw, Sw, few[:, 6, pr:pr + 1], g[:, 2:3], ALU.mult, ALU.mult), sw_p)
                dve.wait_ge(ss_e, pr + 1)
                do(dve.reciprocal(few[:, 10, pr:pr + 1], few[:, 9, pr:pr + 1]))
                do(dve.tensor_scalar(S, S, few[:, 10, pr:pr + 1], g[:, 1:2], ALU.mult, ALU.mult), ss_p)
            meet(dve, 4)
        DVE.append(p4_dve)

        def p4_pool(pool):
            for pr in range(PAIRS):
                for x in (1, 3):
                    if pr >= 1:
                        pool.wait_ge(ss_mm if x < 2 else ss_pv, pr)
                        p4_load_unit(pool, x, 2 * pr + 1)
                for b in range(2):
                    pool.wait_ge(win_in[b], 16 * (pr + 1))
                    pool.dma_start(t["out_win"][2 * pr + b], win[:, b]).then_inc(win_stored, 16)
            pool.wait_ge(win_stored, 16 * NB)
            meet(pool, 4)
        POOL.append(p4_pool)

        def rounds(eng, n, body):
            body(0)
            if n > 1:
                with eng.Fori(1, n) as i:
                    body(i)

        def ring_rounds(sp, name, n, width=SLOT):
            s0, src = slot_at[name], t[name_of[name]]
            with sp.Fori(0, n // RING) as i:
                for j in range(RING):
                    s = s0 + j
                    sp.wait_ge(w_used, i * RING + (s - RING + 1))
                    sp.dma_start(ring[:, s % RING, 0:width], src[bass.ds(i * RING + j, 1)].rearrange("o p n -> (o p) n")
                                 ).then_inc(w_in[s % RING], 16)
            for k in range(n // RING * RING, n):
                s = s0 + k
                sp.wait_ge(w_used, s - RING + 1)
                sp.dma_start(ring[:, s % RING, 0:width], src[k]).then_inc(w_in[s % RING], 16)
        name_of = {"nsa_out": "w_nsa_out", "gu0": "w_gu0", "down0": "w_down0", "ssd_in": "w_ssd_in",
                   "ssd_out": "w_ssd_out", "gu1": "w_gu1", "down1": "w_down1"}

        def in_slot(eng, s, i=0):
            eng.wait_ge(w_in[s % RING], i * 16 + 16 * (s // RING + 1))

        no_ev = sem("nsa_out_taken")

        def p5_sp(sp):
            sp.wait_ge(ss_mm, PAIRS)
            ring_rounds(sp, "nsa_out", 4)
        SP.append(p5_sp)

        def p5_pe(pe):
            s0 = slot_at["nsa_out"]
            for i in range(4):
                in_slot(pe, s0 + i)
                if i >= 2:
                    pe.wait_ge(no_ev, 2 * (i - 1))
                for x in range(2):
                    last = dense(pe, s0 + i, x, 2 * (i % 2) + x, qT)
                last.then_inc(w_used, 1)
        PE.append(p5_pe)

        def p5_dve(dve):
            s0 = slot_at["nsa_out"]
            for m in range(KT):
                dve.wait_ge(w_used, s0 + m // 2 + 1)
                dve_do(dve.tensor_tensor(halves(xT[:, m]), halves(xT[:, m]), pair_ap(m % 4), ALU.add), no_ev)
        DVE.append(p5_dve)

        top[0] = phase_base
        ffn_act = region(FT * NT).rearrange("p (f n) -> p f n", f=FT)
        assert top[0] >= phase_base + KT * NT
        ffn_sq = region(KT * NT).rearrange("p (k n) -> p k n", k=KT)
        ffn_g = region(2 * NT).rearrange("p (x n) -> p x n", x=2)
        ffn_u = region(2 * NT).rearrange("p (x n) -> p x n", x=2)

        g_took, u_took, silu, prod, d_ev = [sem(f"ffn_{n}") for n in (
            "gate_taken", "up_taken", "silu", "product", "down_taken")]

        def swiglu(l, residual):
            norm = Norm((1, 3)[l], (1, 4)[l], PAR["g_ffn"].start + l * KT, ffn_sq, residual)
            f0, x0 = l * FT, l * KT
            s0, d0 = slot_at[f"gu{l}"], slot_at[f"down{l}"]
            full, rest = FT // RING, FT % RING

            def sp_part(sp):
                ring_rounds(sp, f"gu{l}", FT)
                ring_rounds(sp, f"down{l}", 16, 11 * P)

            def pe_part(pe):
                norm.pe(pe)
                norm.wait_scaled(pe)
                norm.wait_root(pe)

                def hidden_tile(i, j):
                    in_slot(pe, s0 + j, i)
                    if not (isinstance(i, int) and i == 0 and j < 2):
                        pe.wait_ge(g_took, i * RING + (f0 + j - 1))
                        pe.wait_ge(u_took, i * RING + (f0 + j - 1))
                    q = 2 * (j % 2)
                    dense(pe, s0 + j, 0, q, hT)
                    dense(pe, s0 + j, 1, q + 1, hT).then_inc(w_used, 1)

                rounds(pe, full, lambda i: [hidden_tile(i, j) for j in range(RING)])
                for j in range(rest):
                    hidden_tile(full, j)
                pe.wait_ge(prod, f0 + FT)

                def down(i):
                    for jj in range(2):
                        if not isinstance(i, int):
                            pe.wait_ge(d_ev, i * 2 + (x0 + jj - 1))
                        for k in range(2):
                            in_slot(pe, d0 + 2 * jj + k, i)
                            last = dense(pe, d0 + 2 * jj + k, 0, jj, ffn_act, kts=11, kt0=11 * k, kt_all=FT)
                            last.then_inc(w_used, 1)
                rounds(pe, 4, down)

            def act_part(act):
                norm.act(act, act_do)

                def hidden_tile(i, j):
                    act.wait_ge(g_took, i * RING + (f0 + j + 1))
                    act.activation(ffn_g[:, j % 2], ffn_g[:, j % 2], ACT.Silu).then_inc(silu, 1)
                rounds(act, full, lambda i: [hidden_tile(i, j) for j in range(RING)])
                for j in range(rest):
                    hidden_tile(full, j)

            def dve_part(dve):
                norm.dve(dve, dve_do)

                def hidden_tile(i, j):
                    f1 = i * RING + (f0 + j + 1)
                    dve.wait_ge(w_used, i * RING + (s0 + j + 1))
                    q, x = 2 * (j % 2), j % 2
                    dve.tensor_tensor(halves(ffn_g[:, x]), pair_ap(q), halves(rstd), ALU.mult).then_inc(g_took, 1)
                    dve.tensor_tensor(halves(ffn_u[:, x]), pair_ap(q + 1), halves(rstd), ALU.mult).then_inc(u_took, 1)
                    dve.wait_ge(u_took, f1)
                    dve.wait_ge(silu, f1)
                    dst = ffn_act[:, i * RING + j] if isinstance(i, int) else \
                        ffn_act[:, bass.ds(i * RING + j, 1)].rearrange("p o n -> p (o n)")
                    dve.tensor_tensor(dst, ffn_g[:, x], ffn_u[:, x], ALU.mult).then_inc(prod, 1)
                    dve.wait_ge(prod, f1)
                rounds(dve, full, lambda i: [hidden_tile(i, j) for j in range(RING)])
                for j in range(rest):
                    hidden_tile(full, j)

                def down(i):
                    for jj in range(2):
                        dve.wait_ge(w_used, i * RING + (d0 + 2 * jj + 2))
                        x = xT[:, jj] if isinstance(i, int) else \
                            xT[:, bass.ds(i * 2 + jj, 1)].rearrange("p o n -> p (o n)")
                        dve.tensor_tensor(halves(x), halves(x), pair_ap(jj), ALU.add).then_inc(d_ev, 1)
                        dve.wait_ge(d_ev, i * 2 + (x0 + jj + 1))
                rounds(dve, 4, down)

            SP.append(sp_part)
            PE.append(pe_part)
            ACTE.append(act_part)
            DVE.append(dve_part)

        swiglu(0, no_ev)
        x1 = d_ev

        top[0] = phase_base
        xc = region(CT * NT).rearrange("p (c n) -> p c n", c=CT)
        zT = region(ST * NT).rearrange("p (c n) -> p c n", c=ST)
        dtT, acT, eacT, teT = [region(NT) for _ in range(4)]
        tok = region(5 * 3 * SH).rearrange("p (c w h) -> p c w h", c=5, w=3)
        cs = region(NSC)
        cs_ = lambda name: cs[:, CONST_S[name]]
        conv_out = region(CT * 27).rearrange("p (c n) -> p c n", c=CT)
        ssd_base = top[0]
        raw = region(2 * RAW).rearrange("p (x n) -> p x n", x=2)
        acc = region(2 * CONV).rearrange("p (x n) -> p x n", x=2)
        ztmp = region(2 * NT).rearrange("p (x n) -> p x n", x=2)
        dv, de, dz, dser = [region(NT) for _ in range(4)]
        neg_a = region(2)
        norm7 = Norm(2, 2, PAR["g_mix"].start + KT, ffn_sq, x1)
        dt_mm, dt_v, dt_exp, dt_a, dt_cum, dt_ecum, dt_ready = [sem(f"dt_{n}") for n in (
            "product", "taken", "exp", "a", "cumsum", "decays", "ready")]
        z_took, z_done = sem("z_taken"), sem("z_done")
        r_state, r_raw, r_last, r_tap, r_conv = [sem(f"conv_{n}") for n in (
            "state", "raw", "last_rows", "first_tap", "summed")]
        d_t = sem("dt_turned")
        conv_w = par[:, PAR["conv_w"]].rearrange("p (c k) -> p c k", c=CT)
        conv_b = par[:, PAR["conv_b"]]
        conv_state = par[:, PAR["conv_state"]].rearrange("p (c b k) -> p c b k", c=CT, b=NB)
        ZS = ST // 2
        XS = CT // 2

        def sample_cols(ap, o):
            return ap[:, SEQ + 3:RAW].rearrange("p (b k) -> p b k", b=NB)[:, :, o:o + 4]

        def p7_sp(sp):
            sp.dma_start(cs, t["const_s"]).then_inc(cs_in, 16)
            ring_rounds(sp, "ssd_in", 20)
        SP.append(p7_sp)

        def p7_pe(pe):
            norm7.pe(pe)
            norm7.wait_scaled(pe)
            w_dt = par[:, PAR["w_dt"]].rearrange("p (k c) -> p k c", k=KT)
            for h in range(2):
                for kt in range(KT):
                    last = pe.matmul(ps[0:SH, 2 + h, 0:HALF], w_dt[:, kt], hT[:, kt, h * HALF:(h + 1) * HALF],
                                     start=kt == 0, stop=kt == KT - 1)
            last.then_inc(dt_mm, 1)
            s0 = slot_at["ssd_in"]
            for i in range(ZS + XS):
                in_slot(pe, s0 + i)
                if i == 0:
                    norm7.wait_root(pe)
                    pe.wait_ge(dt_v, 1)
                elif 2 <= i < ZS + 2:
                    pe.wait_ge(z_took, 2 * (i - 1))
                elif i >= ZS + 2:
                    pe.wait_ge(r_raw, 2 * (i - ZS - 1))
                for x in range(2):
                    last = dense(pe, s0 + i, x, 2 * (i % 2) + x, hT)
                last.then_inc(w_used, 1)
            pe.wait_ge(dt_ready, 1)
            pe.wait_ge(r_raw, CT)
            for c in range(5):
                n, o = (P, c * P) if c < QT else (NS, SEQ)
                for w, src in enumerate((acT, dtT, teT)):
                    last = pe.transpose(ps[0:n, 0, (3 * c + w) * SH:(3 * c + w + 1) * SH], src[0:SH, o:o + n],
                                        ident[0:SH, 0:SH])
            last.then_inc(d_t, 1)
            meet(pe, 5)
        PE.append(p7_pe)

        def p7_act(act):
            do = act_do
            norm7.act(act, do)
            act.wait_ge(dt_v, 1)
            s32 = slice(0, SH)
            for i in range(ZS):
                if i == 1:
                    act.wait_ge(dt_v, 2)
                    do(act.activation(de[s32], dv[s32], ACT.Abs))
                    do(act.activation(de[s32], de[s32], ACT.Exp, scale=-1.0), dt_exp)
                    do(act.activation(neg_a[s32, 0:1], par[s32, PAR["a_log"]], ACT.Exp), dt_a)
                if i == ZS - 1:
                    act.wait_ge(dt_cum, 1)
                    do(act.activation(eacT[s32], acT[s32], ACT.Exp))
                    for c in range(QT):
                        o = c * P
                        do(act.activation(teT[s32, o:o + P], acT[s32, o:o + P], ACT.Exp, scale=-1.0,
                                          bias=acT[s32, o + P - 1:o + P]))
                    for b in range(NB):
                        o = SEQ + b * TS
                        do(act.activation(teT[s32, o:o + TS], acT[s32, o:o + TS], ACT.Exp, scale=-1.0,
                                          bias=acT[s32, o + TS - 1:o + TS]), dt_ecum if b == NB - 1 else None)
                for x in range(2):
                    m = 2 * i + x
                    act.wait_ge(z_took, m + 1)
                    do(act.activation(zT[:, m], ztmp[:, x], ACT.Silu), z_done)
            for i in range(XS):
                for x in range(2):
                    c = 2 * i + x
                    act.wait_ge(r_raw, c + 1)
                    act.wait_ge(r_state, c + 1)
                    do(act.activation(acc[:, x], raw[:, x, 0:CONV], ACT.Identity, bias=conv_b[:, c:c + 1],
                                      scale=conv_w[:, c, 0:1]), r_tap)
                for x in range(2):
                    c = 2 * i + x
                    act.wait_ge(r_conv, c + 1)
                    do(act.activation(xc[:, c, 0:SEQ], acc[:, x, 0:SEQ], ACT.Silu))
                    do(act.activation(xc[:, c, SEQ:NT].rearrange("p (b t) -> p b t", b=NB),
                                      acc_sample(acc[:, x]), ACT.Silu))
            act.wait_ge(d_t, 1)
            do(act.activation(tok[:, 0:QT], ps[:, 0, 0:QT * 96].rearrange("p (c w h) -> p c w h", c=QT, w=3), ACT.Copy))
            do(act.activation(tok[0:NS, QT], ps[0:NS, 0, QT * 96:5 * 96].rearrange("p (w h) -> p w h", w=3), ACT.Copy))
            meet(act, 5)
        ACTE.append(p7_act)

        def acc_sample(ap):
            pad = ap[:, SEQ + 3:CONV]
            return bass.AP(tensor=pad.tensor, offset=pad.offset, ap=[pad.ap[0], [7, NB], [1, TS]])

        def p7_dve(dve):
            do = dve_do
            s32 = slice(0, SH)
            norm7.dve(dve, do)
            dve.wait_ge(dt_mm, 1)
            do(dve.tensor_tensor(halves(dv)[s32], ps[s32, 2:4, 0:HALF], halves(rstd)[s32], ALU.mult), dt_v)
            do(dve.tensor_scalar(dv[s32], dv[s32], par[s32, PAR["dt_bias"]], None, ALU.add), dt_v)
            STEPS = []
            STEPS.append(lambda: (dve.wait_ge(dt_exp, 1), do(dve.tensor_scalar(dz[s32], de[s32], 2.0, None, ALU.add)),
                                  do(dve.reciprocal(dz[s32], dz[s32]))))
            STEPS.append(lambda: (do(dve.tensor_tensor(de[s32], de[s32], dz[s32], ALU.mult)),
                                  do(dve.tensor_tensor(dz[s32], de[s32], de[s32], ALU.mult)),
                                  do(dve.tensor_scalar(dser[s32], dz[s32], 1.0 / 19, None, ALU.mult))))
            for ks in ((8, 7, 6, 5), (4, 3, 2, 1)):
                STEPS.append(lambda ks=ks: [do(dve.scalar_tensor_tensor(
                    dser[s32], dser[s32], 1.0 / (2 * k + 1), dz[s32], ALU.add, ALU.mult)) for k in ks])
            STEPS.append(lambda: (do(dve.scalar_tensor_tensor(dser[s32], dser[s32], 1.0, de[s32], ALU.add, ALU.mult)),
                                  do(dve.tensor_scalar(dv[s32], dv[s32], 0.0, None, ALU.max)),
                                  do(dve.scalar_tensor_tensor(dtT[s32], dser[s32], 2.0, dv[s32], ALU.mult, ALU.add))))
            STEPS.append(lambda: (dve.wait_ge(dt_a, 1), dve.wait_ge(cs_in, 16), do(dve.tensor_scalar(
                teT[s32], dtT[s32], neg_a[s32, 0:1], -1.0, ALU.mult, ALU.mult)), do(dve.tensor_tensor_scan(
                    acT[s32], cs_("keep")[s32], teT[s32], 0.0, ALU.mult, ALU.add), dt_cum)))
            s0 = slot_at["ssd_in"]
            for i in range(ZS):
                dve.wait_ge(w_used, s0 + i + 1)
                for x in range(2):
                    m = 2 * i + x
                    if m >= 2:
                        dve.wait_ge(z_done, m - 1)
                    do(dve.tensor_tensor(halves(ztmp[:, x]), pair_ap(2 * (i % 2) + x), halves(rstd), ALU.mult), z_took)
                if 1 <= i <= len(STEPS):
                    STEPS[i - 1]()
            for i in range(XS):
                dve.wait_ge(w_used, s0 + ZS + i + 1)
                for x in range(2):
                    c = 2 * i + x
                    b0 = 2 * (2 * ((ZS + i) % 2) + x)
                    r = raw[:, x]
                    if c >= 2:
                        dve.wait_ge(r_last, c - 1)
                    else:
                        dve.wait_ge(r_state, 1)
                    do(dve.tensor_tensor(r[:, 3:3 + HALF], ps[:, b0, 0:HALF], rstd[:, 0:HALF], ALU.mult))
                    do(dve.tensor_tensor(r[:, 3 + HALF:3 + SEQ], ps[:, b0 + 1, 0:SEQ - HALF], rstd[:, HALF:SEQ], ALU.mult))
                    do(dve.tensor_tensor(sample_cols(r, 3), ps[:, b0 + 1, SEQ - HALF:HALF].rearrange(
                        "p (b t) -> p b t", b=NB), rstd[:, SEQ:NT].rearrange("p (b t) -> p b t", b=NB), ALU.mult), r_raw)
                for x in range(2):
                    c = 2 * i + x
                    dve.wait_ge(r_tap, c + 1)
                    for k in range(1, 4):
                        do(dve.scalar_tensor_tensor(acc[:, x], raw[:, x, k:k + CONV], conv_w[:, c, k:k + 1], acc[:, x],
                                                    ALU.mult, ALU.add), r_conv if k == 3 else None)
                if i == 0:
                    dve.wait_ge(dt_ecum, 1)
                    do(dve.tensor_tensor(teT[s32], teT[s32], dtT[s32], ALU.mult), dt_ready)
            meet(dve, 5)
        DVE.append(p7_dve)

        def p7_pool(pool):
            pool.wait_ge(x1, KT)
            do = pool_do
            do(pool.memset(raw[:, :, 0:3], 0.0))
            for c in range(CT):
                x = c % 2
                if c >= 2:
                    pool.wait_ge(r_conv, c - 1)
                do(pool.tensor_copy(raw[:, x, SEQ + 3:RAW].rearrange("p (b k) -> p b k", b=NB)[:, :, 0:3],
                                    conv_state[:, c]), r_state)
                pool.wait_ge(r_raw, c + 1)
                do(pool.tensor_copy(conv_out[:, c, 0:3], raw[:, x, SEQ:SEQ + 3]))
                do(pool.tensor_copy(conv_out[:, c, 3:27].rearrange("p (b k) -> p b k", b=NB),
                                    raw[:, x, SEQ + 3:RAW].rearrange("p (b k) -> p b k", b=NB)[:, :, 4:7]), r_last)
            meet(pool, 5)
            pool.dma_start(t["out_conv"], conv_out).then_inc(stored, 16)
        POOL.append(p7_pool)

        top[0] = ssd_base
        state = region(3 * SI).rearrange("p (x c) -> p x c", x=3)
        o1 = ssd_base + SI
        f_sb, off_sb = arena[:, o1:o1 + 512], arena[:, o1 + 512:o1 + 1024]
        o2 = ssd_base + 2 * SI
        seg = arena[:, o2:o2 + 1024].rearrange("p (x n) -> p x n", x=2)
        wgt = arena[:, o2 + 1024:o2 + 2048].rearrange("p (x n) -> p x n", x=2)
        b_tok = region(512)
        e_last = region(12 * SH).rearrange("p (c h) -> p c h", c=12)
        b_own = [region(512), dtT[:, 0:512]]
        e_diag = teT[0:SH, 0:12 * SH].rearrange("p (c h) -> p c h", c=12)
        xdt, xdte = hT_flat[:, 0:SI], hT_flat[:, SI:2 * SI]
        assert top[0] <= 52900
        d_skip = par[:, PAR["d_skip"]]
        ss_names = ("e_diag", "e_product", "e_done", "b_turned", "b_taken", "x_turned", "xdt_done", "cb_done",
                    "spread", "differences", "decays", "weights", "y_product", "y_taken", "off_product",
                    "factor_taken", "off_taken", "y_added", "state_product", "state_scaled", "state_new")
        (e_dg, e_mm, e_done, bt_mm, b_took, xt_mm, xd_took, cb_mm, sg_mm, sg_took, ex_done, w_done, y_mm, y_took,
         of_mm, f_took, o_took, y_added, su_mm, st_scaled, st_new) = [sem(f"scan_{n}") for n in ss_names]
        sa_off, sa_own, sa_fmm = [sem(f"sample_{n}") for n in ("off_product", "own_b", "factor")]
        s_in = [sem(f"state{i}_in") for i in range(2)]
        result_out = sem("results_out")
        TOK_S = slice(SEQ, NT)
        N_CH = QT

        def buf(b):
            return (b + 1) % 2

        def p8_sp(sp):
            load_slots(sp, "ssd_out", t["w_ssd_out"], RING)
            sp.wait_ge(y_added, 4 * (N_CH - 1))
            sp.dma_start(state[:, buf(0)], t["ssm"][0]).then_inc(s_in[buf(0)], 16)
            sp.wait_ge(st_new, 4 * N_CH)
            sp.dma_start(t["out_ssm_p"], state[:, 0]).then_inc(result_out, 16)
            sp.wait_ge(result_out, 16)
            sp.dma_start(state[:, buf(1)], t["ssm"][1]).then_inc(s_in[buf(1)], 16)
            for b in range(NB):
                sp.wait_ge(st_new, 4 * N_CH + 4 * (b + 1))
                sp.dma_start(t["out_ssm_s"][b], state[:, buf(b)]).then_inc(result_out, 16)
                sp.wait_ge(result_out, 16 * (b + 2))
                if b + 2 < NB:
                    sp.dma_start(state[:, buf(b)], t["ssm"][b + 2]).then_inc(s_in[buf(b)], 16)
            s0 = slot_at["ssd_out"]
            for i in range(RING, KT):
                sp.wait_ge(w_used, s0 + i - RING + 1)
                sp.dma_start(ring[:, (s0 + i) % RING], t["w_ssd_out"][i]).then_inc(w_in[(s0 + i) % RING], 16)
        SP.append(p8_sp)

        def turns(pe, c, n, cols):
            if c:
                pe.wait_ge(st_new, 4 * c)
            for g in range(GROUPS):
                last = pe.transpose(ps[0:n, 0, g * P:(g + 1) * P], xc[:, ST + g, cols], ident)
            last.then_inc(bt_mm, 1)
            for k in range(4):
                if k == 1:
                    pe.wait_ge(b_took, c + 1)
                elif k >= 2:
                    pe.wait_ge(xd_took, 4 * c + k - 1)
                for j in range(4):
                    last = pe.transpose(ps[0:n, (k + 1) % 2, j * P:(j + 1) * P], xc[:, 4 * k + j, cols], ident)
                last.then_inc(xt_mm, 1)

        def p8_pe(pe):
            pe.wait_ge(e_dg, 2)
            pe.matmul(ps[:, 7, 0:12 * SH], ones[0:SH], teT[0:SH, 0:12 * SH], start=True, stop=True).then_inc(e_mm, 1)
            for c in range(N_CH):
                cols = slice(c * P, (c + 1) * P)
                turns(pe, c, P, cols)
                if c:
                    pe.wait_ge(w_done, 8 * c)
                for g in range(GROUPS):
                    last = pe.matmul(ps[:, 2, g * P:(g + 1) * P], xc[:, ST + g, cols], xc[:, ST + 4 + g, cols],
                                     start=True, stop=True)
                last.then_inc(cb_mm, 1)
                for k in range(10):
                    if k < 8:
                        if 8 * c + k >= 2:
                            pe.wait_ge(sg_took, 8 * c + k - 1)
                        for j in range(4):
                            h = 4 * k + j
                            last = pe.matmul(ps[:, 3 + k % 2, j * P:(j + 1) * P],
                                             ident[0:SH, h:h + 1].to_broadcast([SH, P]), acT[0:SH, cols],
                                             start=True, stop=True)
                        last.then_inc(sg_mm, 1)
                    if k < 2:
                        continue
                    kk, g = k - 2, (k - 2) // 2
                    if kk % 2 == 0:
                        if c:
                            if c > 1 or g:
                                pe.wait_ge(o_took, 4 * (c - 1) + g)
                                pe.wait_ge(f_took, 4 * (c - 1) + g)
                            else:
                                pe.wait_ge(e_done, 1)
                            for j in range(4):
                                kt = 4 * g + j
                                pe.matmul(ps[:, 6, j * P:(j + 1) * P], state[:, 0, kt * P:(kt + 1) * P],
                                          xc[:, ST + 4 + g, cols], start=True, stop=True)
                                for a in range(2):
                                    h = 2 * kt + a
                                    last = pe.matmul(ps[a * HD:(a + 1) * HD, 7, j * P:(j + 1) * P],
                                                     ident[0:SH, h:h + 1].to_broadcast([SH, HD]), eacT[0:SH, cols],
                                                     start=True, stop=True)
                            last.then_inc(of_mm, 1)
                        if 4 * c + g:
                            pe.wait_ge(y_took, 4 * c + g)
                        pe.wait_ge(xd_took, 4 * c + g + 1)
                    pe.wait_ge(w_done, 8 * c + kk + 1)
                    for j in range(4):
                        h = 4 * kk + j
                        kt, a = h // 2, h % 2
                        last = pe.matmul(ps[a * HD:(a + 1) * HD, 5, (kt % 4) * P:(kt % 4 + 1) * P],
                                         xdt[:, h * HD:(h + 1) * HD], wgt[:, kk % 2, j * P:(j + 1) * P],
                                         start=True, stop=True)
                    last.then_inc(y_mm, 1)
                for g in range(GROUPS):
                    if g >= 2:
                        pe.wait_ge(st_new, 4 * c + g - 1)
                    pe.matmul(ps[:, g % 2], b_tok[:, g * P:(g + 1) * P], xdte[:, g * 512:(g + 1) * 512],
                              start=True, stop=True).then_inc(su_mm, 1)

            turns(pe, N_CH, NS, TOK_S)
            pe.wait_ge(w_done, 8 * N_CH)
            pe.wait_ge(sg_took, 8 * N_CH)
            for g in range(GROUPS):
                pe.matmul(ps[0:NS, 2, g * NS:(g + 1) * NS], xc[:, ST + g, TOK_S], xc[:, ST + 4 + g, TOK_S],
                          start=True, stop=True)
            for h in range(SH):
                last = pe.matmul(ps[0:NS, 3 + h // 16, (h % 16) * NS:(h % 16 + 1) * NS],
                                 ident[0:SH, h:h + 1].to_broadcast([SH, NS]), acT[0:SH, TOK_S], start=True, stop=True)
            last.then_inc(sg_mm, 1)
            pe.wait_ge(f_took, 4 * (N_CH - 1))
            for h in range(SH):
                kt, a = h // 2, h % 2
                last = pe.matmul(ps[a * HD:(a + 1) * HD, 7, kt * NS:(kt + 1) * NS],
                                 ident[0:SH, h:h + 1].to_broadcast([SH, HD]), eacT[0:SH, TOK_S], start=True, stop=True)
            last.then_inc(sa_fmm, 1)
            pe.wait_ge(y_took, 4 * N_CH)
            pe.wait_ge(xd_took, 4 * N_CH + 4)
            pe.wait_ge(w_done, 8 * N_CH + 1)
            for h in range(SH):
                kt, a = h // 2, h % 2
                last = pe.matmul(ps[a * HD:(a + 1) * HD, 5, kt * NS:(kt + 1) * NS], xdt[0:NS, h * HD:(h + 1) * HD],
                                 seg_s[:, h * NS:(h + 1) * NS], start=True, stop=True)
            last.then_inc(y_mm, 1)
            pe.wait_ge(o_took, 4 * (N_CH - 1))
            for b in range(NB):
                pe.wait_ge(s_in[buf(b)], 16 * (b // 2 + 1))
                for kt in range(ST):
                    o = kt * NS + b * TS
                    last = pe.matmul(ps[:, 6, o:o + TS], state[:, buf(b), kt * P:(kt + 1) * P],
                                     xc[:, ST + 4 + kt // 4, SEQ + b * TS:SEQ + (b + 1) * TS], start=True, stop=True)
                last.then_inc(sa_off, 1)
                pe.wait_ge(sa_own, b + 1)
                for g in range(GROUPS):
                    if 4 * b + g >= 2:
                        pe.wait_ge(st_new, 4 * N_CH + 4 * b + g - 1)
                    pe.matmul(ps[:, g % 2], b_own[b % 2][0:NS, g * P:(g + 1) * P],
                              xdte[0:NS, g * 512:(g + 1) * 512], start=True, stop=True).then_inc(su_mm, 1)
        PE.append(p8_pe)

        seg_s = arena[0:NS, o2:o2 + SH * NS]
        f_s, off_s = arena[:, o2 + 1024:o2 + 1536], arena[:, o2 + 1536:o2 + 2048]

        def p8_act(act):
            do = act_do
            act.wait_ge(e_mm, 1)
            do(act.activation(e_last, ps[:, 7, 0:12 * SH].rearrange("p (c h) -> p c h", c=12), ACT.Copy), e_done)
            for c in range(N_CH):
                act.wait_ge(bt_mm, c + 1)
                do(act.activation(b_tok, ps[:, 0], ACT.Copy), b_took)
                for k in range(8):
                    act.wait_ge(sg_took, 8 * c + k + 1)
                    do(act.activation(seg[:, k % 2], seg[:, k % 2], ACT.Exp), ex_done)
                    if c and k % 2:
                        act.wait_ge(of_mm, 4 * (c - 1) + k // 2 + 1)
                        if 4 * (c - 1) + k // 2:
                            act.wait_ge(o_took, 4 * (c - 1) + k // 2)
                        do(act.activation(f_sb, ps[:, 7], ACT.Copy), f_took)
            act.wait_ge(bt_mm, N_CH + 1)
            do(act.activation(b_tok[0:NS], ps[0:NS, 0], ACT.Copy), b_took)
            act.wait_ge(sg_took, 8 * N_CH + 1)
            do(act.activation(seg_s, seg_s, ACT.Exp), ex_done)
            act.wait_ge(sa_fmm, 1)
            act.wait_ge(y_mm, 8 * N_CH)
            do(act.activation(f_s, ps[:, 7], ACT.Copy), f_took)
        ACTE.append(p8_act)

        def p8_dve(dve):
            do = dve_do
            for o, n, at, step in ((0, N_CH, P - 1, P), (N_CH, NB, SEQ + TS - 1, TS)):
                last_cols = eacT[0:SH, at:at + (n - 1) * step + 1:step].rearrange("p (c o) -> p c o", o=1)
                do(dve.tensor_tensor(e_diag[:, o:o + n], ident[0:SH, 0:SH].rearrange("p (o h) -> p o h", o=1)
                                     .to_broadcast([SH, n, SH]), last_cols.to_broadcast([SH, n, SH]), ALU.mult), e_dg)

            def per_head(ap):
                return ap.rearrange("p (h d) -> p h d", d=HD)

            def scaled(c, n):
                for k in range(4):
                    dve.wait_ge(xt_mm, 4 * c + k + 1)
                    for w, dst in ((1, xdt), (2, xdte)):
                        f = tok[0:n, c, w, 8 * k:8 * k + 8].rearrange("p (h o) -> p h o", o=1)
                        do(dve.tensor_tensor(per_head(dst[0:n, k * 512:(k + 1) * 512]),
                                             per_head(ps[0:n, (k + 1) % 2]), f.to_broadcast([n, 8, HD]), ALU.mult),
                           xd_took if w == 2 else None)

            def take_y(c, g):
                cols = slice(c * P, (c + 1) * P)
                dve.wait_ge(y_mm, 8 * c + 2 * g + 2)
                for j in range(4):
                    kt = 4 * g + j
                    do(dve.scalar_tensor_tensor(xc[:, kt, cols], xc[:, kt, cols], d_skip[:, kt:kt + 1],
                                                ps[:, 5, j * P:(j + 1) * P], ALU.mult, ALU.add),
                       y_took if j == 3 else None)
                if c:
                    dve.wait_ge(f_took, 4 * (c - 1) + g + 1)
                    do(dve.tensor_tensor(off_sb, f_sb, ps[:, 6], ALU.mult), o_took)
                    y = xc[:, 4 * g:4 * g + 4, cols]
                    do(dve.tensor_tensor(y, y, off_sb.rearrange("p (k n) -> p k n", k=4), ALU.add), y_added)

            for c in range(N_CH):
                scaled(c, P)
                for k in range(9):
                    if k < 8:
                        dve.wait_ge(sg_mm, 8 * c + k + 1)
                        for j in range(4):
                            h = 4 * k + j
                            do(dve.scalar_tensor_tensor(seg[:, k % 2, j * P:(j + 1) * P],
                                                        ps[:, 3 + k % 2, j * P:(j + 1) * P], tok[:, c, 0, h:h + 1],
                                                        cs_("causal"), ALU.subtract, ALU.add),
                               sg_took if j == 3 else None)
                    if k == 0:
                        dve.wait_ge(cb_mm, c + 1)
                        continue
                    kk = k - 1
                    dve.wait_ge(ex_done, 8 * c + kk + 1)
                    if 8 * c + kk >= 2:
                        dve.wait_ge(y_mm, 8 * c + kk - 1)
                    cb = ps[:, 2, kk // 2 * P:(kk // 2 + 1) * P].rearrange("p (o n) -> p o n", o=1)
                    do(dve.tensor_tensor(wgt[:, kk % 2].rearrange("p (h n) -> p h n", h=4),
                                         seg[:, kk % 2].rearrange("p (h n) -> p h n", h=4),
                                         cb.to_broadcast([P, 4, P]), ALU.mult), w_done)
                    if kk % 2 == 0 and kk:
                        take_y(c, kk // 2 - 1)
                take_y(c, 3)
                for g in range(GROUPS):
                    dve.wait_ge(su_mm, 4 * c + g + 1)
                    st = state[:, 0, g * 512:(g + 1) * 512]
                    if c:
                        dve.wait_ge(st_scaled, c)
                        do(dve.tensor_tensor(st, st, ps[:, g % 2], ALU.add), st_new)
                    else:
                        do(dve.tensor_copy(st, ps[:, g % 2]), st_new)

            scaled(N_CH, NS)
            dve.wait_ge(sg_mm, 8 * N_CH + 1)
            by_head = seg_s.rearrange("p (h n) -> p h n", h=SH)
            acum = tok[0:NS, N_CH, 0].rearrange("p (h o) -> p h o", o=1)
            do(dve.tensor_tensor(by_head, ps[0:NS, 3:5].rearrange("p b (h n) -> p (b h) n", n=NS),
                                 acum.to_broadcast([NS, SH, NS]), ALU.subtract))
            do(dve.tensor_tensor(by_head, by_head, cs_("causal_s")[0:NS].rearrange("p (o n) -> p o n", o=1)
                                 .to_broadcast([NS, SH, NS]), ALU.add), sg_took)
            dve.wait_ge(ex_done, 8 * N_CH + 1)
            cb = ps[0:NS, 2, 0:GROUPS * NS].rearrange("p (g o n) -> p g o n", g=GROUPS, o=1)
            by_group = seg_s.rearrange("p (g h n) -> p g h n", g=GROUPS, h=8)
            do(dve.tensor_tensor(by_group, by_group, cb.to_broadcast([NS, GROUPS, 8, NS]), ALU.mult), w_done)
            for b in range(NB):
                for g in range(GROUPS):
                    dve.wait_ge(su_mm, 4 * N_CH + 4 * b + g + 1)
                    dve.wait_ge(st_scaled, N_CH - 1 + b + 1)
                    st = state[:, buf(b), g * 512:(g + 1) * 512]
                    do(dve.tensor_tensor(st, st, ps[:, g % 2], ALU.add), st_new)
            dve.wait_ge(y_mm, 8 * N_CH + 1)
            y = xc[:, 0:ST, TOK_S]
            by_tile = lambda ap: ap.rearrange("p (k n) -> p k n", k=ST)
            do(dve.tensor_tensor(y, y, d_skip.rearrange("p (k o) -> p k o", o=1).to_broadcast([P, ST, NS]), ALU.mult))
            do(dve.tensor_tensor(y, y, by_tile(ps[:, 5]), ALU.add))
            dve.wait_ge(f_took, 4 * (N_CH - 1) + 1)
            do(dve.tensor_tensor(off_s, f_s, ps[:, 6], ALU.mult))
            do(dve.tensor_tensor(y, y, by_tile(off_s), ALU.add))
        DVE.append(p8_dve)

        def p8_pool(pool):
            do = pool_do

            def decayed(st, c, signal):
                ap = st.rearrange("p (h d) -> p h d", d=HD)
                e = e_last[:, c].rearrange("p (h o) -> p h o", o=1)
                do(pool.tensor_tensor(ap, ap, e.to_broadcast([P, SH, HD]), ALU.mult), signal)

            pool.wait_ge(e_done, 1)
            for c in range(1, N_CH):
                pool.wait_ge(of_mm, 4 * c)
                decayed(state[:, 0], c, st_scaled)
            pool.wait_ge(b_took, N_CH + 1)
            for b in range(NB):
                if b >= 2:
                    pool.wait_ge(su_mm, 4 * N_CH + 4 * (b - 1))
                do(pool.tensor_scalar(b_own[b % 2][0:NS], b_tok[0:NS], cs_("own")[0:NS, b:b + 1], None, ALU.mult),
                   sa_own)
                pool.wait_ge(sa_off, b + 1)
                decayed(state[:, buf(b)], N_CH + b, st_scaled)
        POOL.append(p8_pool)

        g_gated, g_sq, g_sp, g_out = [sem(f"gated_{n}") for n in ("product", "squared", "spread", "normed")]
        SQ = zT
        ssm_norm = par[:, PAR["ssm_norm"]]
        y1 = sem("ssd_out_taken")

        def p9_dve(dve):
            do = dve_do
            for j in range(ST):
                do(dve.tensor_tensor(xc[:, j], xc[:, j], zT[:, j], ALU.mult), g_gated)
            dve.wait_ge(n_rt, 4)
            do(dve.reciprocal(rstd[0:GROUPS], rstd[0:GROUPS]), n_r)
            for j in range(ST):
                dve.wait_ge(g_sp, j // 4 + 1)
                do(dve.scalar_tensor_tensor(halves(xc[:, j]), halves(xc[:, j]), ssm_norm[:, j:j + 1], pair_ap(j // 4),
                                            ALU.mult, ALU.mult), g_out)
            s0 = slot_at["ssd_out"]
            for m in range(KT):
                dve.wait_ge(w_used, s0 + m + 1)
                do(dve.tensor_tensor(halves(xT[:, m]), halves(xT[:, m]), pair_ap(m % 4), ALU.add), y1)
        DVE.append(p9_dve)

        def p9_act(act):
            do = act_do
            for j in range(ST):
                act.wait_ge(g_gated, j + 1)
                do(act.activation(SQ[:, j], xc[:, j], ACT.Square), g_sq)
            act.wait_ge(n_ss, 4)
            do(act.activation(halves(rstd)[0:GROUPS], ps[0:GROUPS, 0:2, 0:HALF], ACT.Sqrt, bias=eps[0:GROUPS],
                              scale=float(GROUPS) / SI), n_rt)
        ACTE.append(p9_act)

        def p9_pe(pe):
            pe.wait_ge(st_new, 4 * N_CH + 4 * NB)
            for j in range(ST):
                pe.wait_ge(g_sq, j + 1)
                g = j // 4
                for h in range(2):
                    last = pe.matmul(ps[0:GROUPS, h, 0:HALF], onecol[:, 3 - g:7 - g], SQ[:, j, h * HALF:(h + 1) * HALF],
                                     start=j == 0, stop=j == ST - 1)
            last.then_inc(n_ss, 1)
            pe.wait_ge(n_r, 4)
            for g in range(GROUPS):
                for h in range(2):
                    last = pe.matmul(ps[:, 2 * g + h, 0:HALF], ident[0:GROUPS, g:g + 1].to_broadcast([GROUPS, P]),
                                     rstd[0:GROUPS, h * HALF:(h + 1) * HALF], start=True, stop=True)
                last.then_inc(g_sp, 1)
            s0 = slot_at["ssd_out"]
            for m in range(KT):
                in_slot(pe, s0 + m)
                if m == 0:
                    pe.wait_ge(g_out, ST)
                elif m >= 4:
                    pe.wait_ge(y1, m - 3)
                dense(pe, s0 + m, 0, m % 4, xc, kts=ST).then_inc(w_used, 1)
        PE.append(p9_pe)

        swiglu(1, y1)

        def out_sp(sp):
            for m in range(KT):
                sp.wait_ge(d_ev, KT + m + 1)
                sp.dma_start(t["out_x"][:, m], xT[:, m]).then_inc(result_out, 16)
            sp.wait_ge(result_out, 16 * (1 + NB + KT))
        SP.append(out_sp)

        act_do, dve_do, pool_do = None, None, None

        @block.sync
        def _(sp):
            for part in SP:
                part(sp)

        @block.tensor
        def _(pe):
            for part in PE:
                part(pe)

        @block.scalar
        def _(act):
            nonlocal act_do
            act_do = InOrder(act, act_own)
            for part in ACTE:
                part(act)

        @block.vector
        def _(dve):
            nonlocal dve_do
            dve_do = InOrder(dve, dve_own)
            for part in DVE:
                part(dve)

        @block.gpsimd
        def _(pool):
            nonlocal pool_do
            pool_do = InOrder(pool, pool_own)
            for part in POOL:
                part(pool)
            pool.wait_ge(stored, 16 * 2)


def kt_major(w, n_tiles):
    k = w.shape[0]
    return w.reshape(k // P, P, n_tiles, P).transpose(2, 1, 0, 3)


def slots_of(w, n_tiles):
    m = kt_major(w, n_tiles)
    m = m.reshape(n_tiles // 2, 2, P, m.shape[2] * P).transpose(0, 2, 1, 3)
    return np.ascontiguousarray(m.reshape(n_tiles // 2, P, -1))


def arrays(x_prompt, x_sample, cache_kv_cmp, cache_kv_sel, cache_kv_win, state_conv, state_ssm, page_table,
           norm_mix, norm_ffn, nsa_w_in, nsa_qk_gain, nsa_cmp_pe, nsa_cmp_w1, nsa_cmp_w2, nsa_w_out,
           ssd_w_in, ssd_conv_w, ssd_conv_b, ssd_dt_bias, ssd_a_log, ssd_d, ssd_norm, ssd_w_out,
           ffn_w_gate, ffn_w_up, ffn_w_down):
    a = {}
    x = np.concatenate([x_prompt[0], x_sample.reshape(NS, D)])
    a["x"] = x.T.reshape(KT, P, NT).transpose(1, 0, 2)
    w = nsa_w_in[0]
    order = [head_of(kt, h) for kt in range(KT) for h in range(2)]
    wq = w[:, :D].reshape(D, HEADS, HD)[:, order].reshape(D, D)
    a["w_nsa_in"] = slots_of(np.concatenate([wq, w[:, D:D + 1536]], 1), 20)
    a["w1"] = np.ascontiguousarray(
        nsa_cmp_w1[0].reshape(2, 2, 8, P, 256).transpose(0, 3, 1, 2, 4)).reshape(2, P, 2, SLOT).transpose(0, 2, 1, 3).reshape(4, P, SLOT)
    wo = nsa_w_out[0].reshape(HEADS, HD, D)[order].reshape(D, D)
    a["w_nsa_out"] = slots_of(wo, 8)
    for l in range(2):
        g, u = kt_major(ffn_w_gate[l], FT), kt_major(ffn_w_up[l], FT)
        a[f"w_gu{l}"] = np.stack([g, u], 2).reshape(FT, P, SLOT)
        dn = kt_major(ffn_w_down[l], KT)
        a[f"w_down{l}"] = dn.reshape(KT, P, 2, 11 * P).transpose(0, 2, 1, 3).reshape(16, P, 11 * P)
    w = ssd_w_in[0]
    a["w_ssd_in"] = slots_of(w[:, :5120], 40)
    a["w_ssd_out"] = kt_major(ssd_w_out[0], KT).reshape(KT, P, SLOT)
    par = np.zeros((P, NPAR), np.float32)

    def put(name, v, rows=P):
        par[:rows, PAR[name]] = v

    put("g_mix", norm_mix.reshape(2 * KT, P).T)
    put("g_ffn", norm_ffn.reshape(2 * KT, P).T)
    put("qk", np.concatenate([nsa_qk_gain[0].T] * 2))
    put("pe", nsa_cmp_pe[0].reshape(2, 2, KT, P).transpose(3, 0, 1, 2).reshape(P, -1))
    put("w2", nsa_cmp_w2[0].reshape(2, 2, P, HD).transpose(2, 0, 1, 3).reshape(P, -1))
    put("w_gate", nsa_w_in[0][:, D + 1536:].reshape(KT, P, 48).transpose(1, 0, 2).reshape(P, -1))
    put("w_dt", w[:, 5120:].reshape(KT, P, SH).transpose(1, 0, 2).reshape(P, -1))
    put("conv_w", ssd_conv_w[0].reshape(4, CT, P).transpose(2, 1, 0).reshape(P, -1))
    put("conv_b", ssd_conv_b[0].reshape(CT, P).T)
    put("d_skip", np.repeat(ssd_d[0].reshape(ST, 2), HD, 1).T)
    put("ssm_norm", ssd_norm[0].reshape(ST, P).T)
    put("a_log", ssd_a_log[0][:, None], SH)
    put("dt_bias", ssd_dt_bias[0][:, None], SH)
    put("conv_state", state_conv[0].reshape(NB, 3, CT, P).transpose(3, 2, 0, 1).reshape(P, -1))
    a["par"] = par
    a["const_a"], a["const_n"], a["const_ali"], a["const_s"] = const_a(), const_n(), const_ali(), const_s()
    a["pages"] = page_table.reshape(1, -1)
    c = cache_kv_cmp[0].reshape(NPHYS, 8, 8, 2, 2, GROUPS, HD)
    a["cmp_pages"] = c.transpose(0, 4, 3, 6, 5, 2, 1).reshape(NPHYS, 2, P, 256)
    c = cache_kv_sel[0]
    a["sel_k"] = c[:, :, 0].reshape(NPHYS, PAGE, 2, 2 * HD).transpose(0, 3, 2, 1).reshape(NPHYS, P, 256)
    a["sel_v"] = c[:, :, 1].reshape(NPHYS, PAGE, 256)
    c = cache_kv_win[0]
    wk = c[:, :, 0].reshape(NB, SEQ, 2, P).transpose(0, 3, 2, 1).reshape(NB, P, 1024)
    wv = c[:, :, 1].reshape(NB, QT, P, 256).transpose(0, 2, 1, 3).reshape(NB, P, 1024)
    a["win"] = np.concatenate([wk, wv], 2)
    s = state_ssm[0].reshape(NB, SI, P)
    a["ssm"] = s.transpose(0, 2, 1)
    return {k: np.ascontiguousarray(v) for k, v in a.items()}


OUTS = {
    "out_kv": (P, 12, NT), "out_conv": (P, CT, 27), "out_win": (NB, P, 2048),
    "out_ssm_p": (P, SI), "out_ssm_s": (NB, P, SI), "out_x": (P, KT, NT),
}


def returned(r):
    y = r["out_x"].transpose(2, 1, 0).reshape(NT, D)
    kv = r["out_kv"].reshape(2, HD, 6, 2, NT).transpose(4, 2, 3, 0, 1).reshape(NT, 6, GROUPS, HD)
    branch = {n: np.stack([kv[:, k], kv[:, v]], 1) for n, k, v in (("cmp", 0, 1), ("sel", 4, 2), ("win", 5, 3))}
    new = {n: b[SEQ:].reshape(1, NB, TS, 2, GROUPS, HD) for n, b in branch.items()}
    old = {n: b[:SEQ].reshape(1, 1, SEQ, 2, GROUPS, HD) for n, b in branch.items()}
    w = r["out_win"]
    k = w[:, :, :1024].reshape(NB, P, 2, SEQ).transpose(0, 3, 2, 1).reshape(NB, SEQ, GROUPS, HD)
    v = w[:, :, 1024:].reshape(NB, P, QT, 256).transpose(0, 2, 1, 3).reshape(NB, SEQ, GROUPS, HD)
    win = np.concatenate([np.stack([k, v], 2)[None, :, TS:], new["win"]], 2)
    conv = r["out_conv"].transpose(2, 1, 0).reshape(27, CT * P)
    ssm = lambda a: np.ascontiguousarray(np.swapaxes(a, -1, -2)).reshape(1, -1, SH, HD, P)
    outs = (y[:SEQ][None], y[SEQ:].reshape(NB, TS, D), old["cmp"], old["sel"], old["win"], conv[None, None, :3],
            ssm(r["out_ssm_p"]), new["cmp"], new["sel"], win, conv[3:].reshape(1, NB, 3, -1), ssm(r["out_ssm_s"]))
    return tuple(np.ascontiguousarray(o) for o in outs)


def kernel(**inputs):
    import concourse.bacc as bacc
    from concourse.bass_utils import run_bass_kernel_spmd as run
    nc = bacc.Bacc("TRN2", target_bir_lowering=False, num_devices=1)
    arr = arrays(**{k: np.asarray(v) for k, v in inputs.items()})
    t = {k: nc.dram_tensor(k, v.shape, mybir.dt.from_np(v.dtype), kind="ExternalInput").ap() for k, v in arr.items()}
    t |= {k: nc.dram_tensor(k, s, F32, kind="ExternalOutput").ap() for k, s in OUTS.items()}
    build(nc, t)
    r = run(nc, [arr], core_ids=[0]).results[0]
    return returned(r)
```
